# Optimizing a Trainium2 kernel written in Bass

```python
import math
import jax, jax.numpy as jnp
from jax import lax
import numpy as np

D_MODEL = 2048
BATCH = 1
SEQ = 256
DEPTH = 1

N_META = 16
N_MIXERS = 2
MIX_WIDTH = D_MODEL
RMS_EPS = 1e-6
S5_GROUP = 16
S5_GROUPS = MIX_WIDTH // S5_GROUP
S5_STATE = 64
S5_CHUNK = 128
DT_MIN = 1e-3
DT_MAX = 1e-1
POOL_WINDOWS = (2, 4, 8, 16)
POOL_GROUPS = len(POOL_WINDOWS)
POOL_GROUP_WIDTH = MIX_WIDTH // POOL_GROUPS
N_EXPERT_GROUPS = 4
EXPERTS_PER_GROUP = 8
N_EXPERTS = N_EXPERT_GROUPS * EXPERTS_PER_GROUP
TOP_K_INNER = 2
D_EXPERT = D_MODEL // 4

kernel_name = 'hybrid_s5_pool_hmoe_trunk'

F32 = jnp.float32

def rms_norm(h, g):
    hf = h.astype(F32)
    y = hf * lax.rsqrt(jnp.mean(hf * hf, axis=-1, keepdims=True) + RMS_EPS) * g.astype(F32)
    return y.astype(h.dtype)

def s5_mixer(h, w_in, a_re, a_im, log_dt, b_re, b_im, c_re, c_im, d_skip, w_glu):
    bsz, t_len, _ = h.shape
    u = (h @ w_in).astype(F32).reshape(bsz, t_len, S5_GROUPS, S5_GROUP)
    dt = jnp.exp(log_dt.astype(F32))[:, None]
    lr, li = a_re.astype(F32), a_im.astype(F32)
    mag = jnp.exp(lr * dt)
    abar_re = mag * jnp.cos(li * dt)
    abar_im = mag * jnp.sin(li * dt)
    den = lr * lr + li * li
    nr, ni = abar_re - 1.0, abar_im
    coef_re = (nr * lr + ni * li) / den
    coef_im = (ni * lr - nr * li) / den
    br, bi = b_re.astype(F32), b_im.astype(F32)
    bbar_re = coef_re[..., None] * br - coef_im[..., None] * bi
    bbar_im = coef_re[..., None] * bi + coef_im[..., None] * br
    cr, ci = c_re.astype(F32), c_im.astype(F32)

    def combine(e1, e2):
        a1r, a1i, b1r, b1i = e1
        a2r, a2i, b2r, b2i = e2
        return (a1r * a2r - a1i * a2i, a1r * a2i + a1i * a2r,
                a2r * b1r - a2i * b1i + b2r, a2r * b1i + a2i * b1r + b2i)

    def chunk_scan(u_c, h0_re, h0_im):
        bu_re = jnp.einsum('blgh,gph->blgp', u_c, bbar_re)
        bu_im = jnp.einsum('blgh,gph->blgp', u_c, bbar_im)
        ar = jnp.broadcast_to(abar_re, bu_re.shape)
        ai = jnp.broadcast_to(abar_im, bu_re.shape)
        pr, pi, sr, si = lax.associative_scan(combine, (ar, ai, bu_re, bu_im), axis=1)
        xr = sr + pr * h0_re[:, None] - pi * h0_im[:, None]
        xi = si + pr * h0_im[:, None] + pi * h0_re[:, None]
        y = jnp.einsum('blgp,ghp->blgh', xr, cr) - jnp.einsum('blgp,ghp->blgh', xi, ci)
        return y, xr[:, -1], xi[:, -1]

    zeros = jnp.zeros((bsz, S5_GROUPS, S5_STATE), F32)
    y_meta, h_re, h_im = chunk_scan(u[:, :N_META], zeros, zeros)
    n_chunks = (t_len - N_META) // S5_CHUNK
    u_real = u[:, N_META:].reshape(bsz, n_chunks, S5_CHUNK, S5_GROUPS, S5_GROUP)
    u_real = jnp.moveaxis(u_real, 1, 0)

    def body(carry, u_c):
        y_c, hr, hi = chunk_scan(u_c, carry[0], carry[1])
        return (hr, hi), y_c

    _, y_chunks = lax.scan(body, (h_re, h_im), u_real)
    y_real = jnp.moveaxis(y_chunks, 0, 1).reshape(bsz, t_len - N_META, S5_GROUPS, S5_GROUP)
    y = jnp.concatenate([y_meta, y_real], axis=1)
    y = y + d_skip.astype(F32).reshape(S5_GROUPS, S5_GROUP) * u
    z = jax.nn.gelu(y.reshape(bsz, t_len, MIX_WIDTH))
    vg = z @ w_glu
    out = vg[..., :D_MODEL] * jax.nn.sigmoid(vg[..., D_MODEL:])
    return out.astype(h.dtype)

def pool_mixer(h, w_in, w_grp, scale):
    bsz, t_len, _ = h.shape
    u = (h @ w_in).astype(F32).reshape(bsz, t_len, POOL_GROUPS, POOL_GROUP_WIDTH)
    cs = jnp.cumsum(u, axis=1)
    t_idx = jnp.arange(t_len)
    pooled = []
    for g, w in enumerate(POOL_WINDOWS):
        csg = cs[:, :, g]
        lag = jnp.pad(csg, ((0, 0), (w, 0), (0, 0)))[:, :t_len]
        cnt = jnp.minimum(t_idx + 1, w).astype(F32)[None, :, None]
        pooled.append((csg - lag) / cnt)
    pooled = jnp.stack(pooled, axis=2)
    mixed = pooled - u
    y = jnp.einsum('btgc,gcd->btgd', mixed, w_grp.astype(F32)).reshape(bsz, t_len, D_MODEL)
    return (y * scale.astype(F32)).astype(h.dtype)

def hier_moe(h, w_coarse, b_coarse, w_fine, b_fine, w_gate, w_up, w_down):
    bsz, t_len, d = h.shape
    xt = h.reshape(-1, d)
    n_tok = xt.shape[0]
    coarse_p = jax.nn.softmax((xt @ w_coarse).astype(F32) + b_coarse.astype(F32), axis=-1)
    p_grp, grp = lax.top_k(coarse_p, 1)
    fine_logits = ((xt @ w_fine).astype(F32) + b_fine.astype(F32)).reshape(n_tok, N_EXPERT_GROUPS, EXPERTS_PER_GROUP)
    idx = jnp.broadcast_to(grp[:, :, None], (n_tok, 1, EXPERTS_PER_GROUP))
    fine_sel = jnp.take_along_axis(fine_logits, idx, axis=1)[:, 0]
    p_exp, exp_local = lax.top_k(jax.nn.softmax(fine_sel, axis=-1), TOP_K_INNER)
    w_exp = p_exp / jnp.sum(p_exp, axis=-1, keepdims=True) * p_grp
    exp_idx = grp * EXPERTS_PER_GROUP + exp_local
    gates = jnp.sum(jax.nn.one_hot(exp_idx, N_EXPERTS, dtype=F32) * w_exp[..., None], axis=1)
    out = jnp.zeros((n_tok, d), F32)
    for e in range(N_EXPERTS):
        hid = jax.nn.silu(xt @ w_gate[e]) * (xt @ w_up[e])
        out = out + gates[:, e:e + 1] * (hid @ w_down[e]).astype(F32)
    return out.astype(h.dtype).reshape(bsz, t_len, d)

def setup_inputs(seed: int = 0) -> dict:
    key = jax.random.key(seed)
    ks = iter(jax.random.split(key, 40))
    n_a = (DEPTH + N_MIXERS - 1) // N_MIXERS
    n_b = DEPTH // N_MIXERS

    def nrm(shape, scale):
        return jax.random.normal(next(ks), shape, F32) * scale

    ns = jnp.arange(S5_STATE, dtype=F32)
    return {
        'x': nrm((BATCH, SEQ, D_MODEL), 1.0),
        'meta_tokens': nrm((N_META, D_MODEL), 1.0),
        'norm_mix': 1.0 + nrm((DEPTH, D_MODEL), 0.02),
        'norm_ffn': 1.0 + nrm((DEPTH, D_MODEL), 0.02),
        'norm_final': 1.0 + nrm((D_MODEL,), 0.02),
        's5_w_in': nrm((n_a, D_MODEL, MIX_WIDTH), D_MODEL ** -0.5),
        's5_a_re': -0.5 + nrm((n_a, S5_GROUPS, S5_STATE), 0.01),
        's5_a_im': jnp.pi * ns + nrm((n_a, S5_GROUPS, S5_STATE), 0.01),
        's5_log_dt': jax.random.uniform(next(ks), (n_a, S5_GROUPS), F32, math.log(DT_MIN), math.log(DT_MAX)),
        's5_b_re': nrm((n_a, S5_GROUPS, S5_STATE, S5_GROUP), (2 * S5_GROUP) ** -0.5),
        's5_b_im': nrm((n_a, S5_GROUPS, S5_STATE, S5_GROUP), (2 * S5_GROUP) ** -0.5),
        's5_c_re': nrm((n_a, S5_GROUPS, S5_GROUP, S5_STATE), S5_STATE ** -0.5),
        's5_c_im': nrm((n_a, S5_GROUPS, S5_GROUP, S5_STATE), S5_STATE ** -0.5),
        's5_d': nrm((n_a, MIX_WIDTH), 1.0),
        's5_w_glu': nrm((n_a, MIX_WIDTH, 2 * D_MODEL), MIX_WIDTH ** -0.5),
        'pool_w_in': nrm((n_b, D_MODEL, MIX_WIDTH), D_MODEL ** -0.5),
        'pool_w_grp': nrm((n_b, POOL_GROUPS, POOL_GROUP_WIDTH, POOL_GROUP_WIDTH), POOL_GROUP_WIDTH ** -0.5),
        'pool_scale': 1.0 + nrm((n_b, D_MODEL), 0.02),
        'moe_w_coarse': nrm((DEPTH, D_MODEL, N_EXPERT_GROUPS), D_MODEL ** -0.5),
        'moe_b_coarse': nrm((DEPTH, N_EXPERT_GROUPS), 0.01),
        'moe_w_fine': nrm((DEPTH, D_MODEL, N_EXPERTS), D_MODEL ** -0.5),
        'moe_b_fine': nrm((DEPTH, N_EXPERTS), 0.01),
        'moe_w_gate': nrm((DEPTH, N_EXPERTS, D_MODEL, D_EXPERT), D_MODEL ** -0.5),
        'moe_w_up': nrm((DEPTH, N_EXPERTS, D_MODEL, D_EXPERT), D_MODEL ** -0.5),
        'moe_w_down': nrm((DEPTH, N_EXPERTS, D_EXPERT, D_MODEL), D_EXPERT ** -0.5),
    }

def reference(x, meta_tokens, norm_mix, norm_ffn, norm_final,
              s5_w_in, s5_a_re, s5_a_im, s5_log_dt, s5_b_re, s5_b_im, s5_c_re, s5_c_im, s5_d, s5_w_glu,
              pool_w_in, pool_w_grp, pool_scale,
              moe_w_coarse, moe_b_coarse, moe_w_fine, moe_b_fine, moe_w_gate, moe_w_up, moe_w_down):
    bsz = x.shape[0]
    meta = jnp.broadcast_to(meta_tokens[None].astype(x.dtype), (bsz, N_META, D_MODEL))
    h = jnp.concatenate([meta, x], axis=1)
    for i in range(DEPTH):
        hn = rms_norm(h, norm_mix[i])
        j = i // N_MIXERS
        if i % N_MIXERS == 0:
            h = h + s5_mixer(hn, s5_w_in[j], s5_a_re[j], s5_a_im[j], s5_log_dt[j], s5_b_re[j], s5_b_im[j],
                             s5_c_re[j], s5_c_im[j], s5_d[j], s5_w_glu[j])
        else:
            h = h + pool_mixer(hn, pool_w_in[j], pool_w_grp[j], pool_scale[j])
        h = h + hier_moe(rms_norm(h, norm_ffn[i]), moe_w_coarse[i], moe_b_coarse[i], moe_w_fine[i],
                         moe_b_fine[i], moe_w_gate[i], moe_w_up[i], moe_w_down[i])
    h = rms_norm(h, norm_final)
    return h[:, N_META:]


_drawn_inputs = setup_inputs


def setup_inputs(seed=0):
    import zlib

    import numpy as np

    out = dict(_drawn_inputs(seed))
    spreads = {}
    factors = {'meta_tokens': 200.0,
     'norm_final': 23.452,
     's5_a_re': 200.0,
     'moe_b_coarse': 20.139,
     'moe_b_fine': 8.0,
     'norm_mix': 3.099,
     's5_log_dt': 2.779,
     's5_b_re': 12.328,
     's5_b_im': 18.22,
     's5_c_re': 10.898,
     's5_c_im': 10.987,
     'norm_ffn': 2.834,
     's5_a_im': 2.949}
    for name, (base, spread) in spreads.items():
        noise = np.random.default_rng([zlib.crc32(name.encode()), seed]).standard_normal(out[name].shape)
        drawn = base * np.exp(spread * noise) if base else spread * noise
        out[name] = __import__('jax').numpy.asarray(drawn.astype(out[name].dtype))
    for name, factor in factors.items():
        out[name] = (out[name] * factor).astype(out[name].dtype)
    return out
```

```python
from contextlib import ExitStack
import math

import concourse.bass as bass
from concourse import mybir

F32 = mybir.dt.float32
I32 = mybir.dt.int32
U32 = mybir.dt.uint32
ALU = mybir.AluOpType
ACT = mybir.ActivationFunctionType
AX = mybir.AxisListType

P = 128
D = 2048
KT = D // P
META = 16
SEQ = 256
T = META + SEQ
L = 8
C = T // L
MC = META // L
G = 128
H = 16
NS = 64
GT = P // H
TR = [3 * C, 3 * C, 2 * C]
TO = [0, 3 * C, 6 * C]
R = TR[0]
E = 32
EG = 4
EL = 8
FE = 512
FT = FE // P
SL = 64
NPASS = -(-T // SL)
NPAIR = E // 2
UNIT = 4096
EPS = 1e-6
ROUND = 12582912.0
TWO_PI = 6.2831845
INV_2PI = 1.0 / (2.0 * math.pi)
EXP_FLOOR = -32.0


def trunk(nc, a, out):
    ctx = ExitStack()
    with ctx:
        arena = ctx.enter_context(nc.sbuf_tensor("arena", [P, 53200], F32))
        count_sb = ctx.enter_context(nc.sbuf_tensor("count_sb", [1, 1], I32))
        bank = [ctx.enter_context(nc.psum_tensor(f"bank{i}", [P, 512], F32)) for i in range(8)]

        def sem(name):
            return ctx.enter_context(nc.semaphore(name))

        def at(base, *dims):
            n = 1
            for d in dims:
                n *= d
            v = arena[:, base:base + n]
            if len(dims) == 1:
                return v
            names = "abcd"[:len(dims)]
            return v.rearrange(f"p ({' '.join(names)}) -> p {' '.join(names)}",
                               **{names[i]: dims[i] for i in range(1, len(dims))})

        def carver(base, end):
            pos = [base]

            def carve(*dims):
                v = at(pos[0], *dims)
                for_size = 1
                for d in dims:
                    for_size *= d
                pos[0] += for_size
                assert pos[0] <= end, (pos[0], end)
                return v
            return carve

        RING, RES = 0, 8 * UNIT
        REG2 = RES + KT * T
        REG3 = REG2 + 3 * D
        CONST = 53200 - 512
        slot = [at(RING + i * UNIT, UNIT) for i in range(8)]
        hT = at(RES, KT, T)

        const = carver(CONST, 53200)
        ident = const(P)
        iota = const(SL)
        notfirst = const(C)
        turn = const(P)
        g_mix = const(KT)
        g_ffn = const(KT)
        d_skip = const(KT)
        stat = const(12)
        round_c, quarter = const(1), const(1)
        stat3 = [stat[0:R, 3 * i:3 * i + 3] for i in range(4)]

        s5a = carver(RING + 4 * UNIT, RING + 8 * UNIT)
        b1, b2, c1, c2 = s5a(H, G), s5a(H, G), s5a(H, G), s5a(H, G)
        hsT = s5a(KT, T)
        pow_re, pow_im = s5a(L + 1, G), s5a(L + 1, G)
        rho8, phi8 = s5a(G), s5a(G)
        u_sb = [s5a(T) for _ in range(2)]
        u_ch = [s5a(GT, C) for _ in range(2)]

        s5b = carver(RING + 2 * UNIT, RING + 4 * UNIT)
        w_tmp, g_tmp = s5b(GT, L + 1, H), s5b(GT, L, H)
        cos_t = [s5b(GT, C) for _ in range(2)]
        sin_t = [s5b(GT, C) for _ in range(2)]
        mag_t = [s5b(GT, C) for _ in range(2)]
        frac, whole = s5b(GT, C), s5b(GT, C)
        s_sb, t1, t2, zz = s5b(GT, C), s5b(GT, C), s5b(GT, C), s5b(GT, C)
        x_prev = s5b(GT, C + 1)
        y_sb = s5b(GT, C)
        y_ch = [s5b(T) for _ in range(2)]
        diag = s5b(3, R)
        small = [s5b(NS) for _ in range(16)]

        nat = carver(REG3, CONST)
        b_raw = nat(2, NS, H)
        b_nat = nat(3, NS, H)
        c_nat = nat(H, 3, NS)
        nat4 = nat(4, 2, NS)
        p_tmp = nat(4, G)

        s5c = carver(REG3, CONST)
        w_sb = [s5c(GT, L + 1, H) for _ in range(2)]
        g_sb, gt_sb, t_sb = s5c(GT, L, H), s5c(GT, P), s5c(GT, L, H)
        b_rep = s5c(GT, L + 1, H)
        u_ch += [s5c(GT, C) for _ in range(2)]

        h_nat = at(REG2, 3, D)
        zT = at(REG2, KT, T)
        glu = carver(REG2 + KT * T, REG3)
        w_router = glu(KT, EG + E)
        b_router = glu(EG + E)
        sumsq = glu(3, KT)

        moe = carver(REG3, CONST)
        xn = moe(3, D)
        h_new = [moe(T) for _ in range(2)]
        gate_s = [moe(T) for _ in range(2)]
        value_s = moe(T)
        rank = moe(E, 3)
        gates = moe(E, 3)
        square_s = moe(P)
        moe2 = carver(REG3 + 3 * D, REG3 + 3 * D + 5 * T)
        pick, pick_g = moe2(3, 2, SL), moe2(3, 2, SL)
        pick_t = [moe(T) for _ in range(2)]

        rt = carver(REG2, REG2 + KT * T)
        logit = rt(3, EG + E)
        coarse, fine_sel = rt(3, EL), rt(3, EL)
        prod = rt(3, EL, EG)
        cmax, fmax = rt(3, 8), rt(3, 8)
        cidx, fidx = rt(3, 8).bitcast(U32), rt(3, 8).bitcast(U32)
        one4, ex4 = rt(3, EG), rt(3, EG)
        col = [rt(3) for _ in range(12)]
        hot = [rt(E, 3) for _ in range(3)]
        before, ones = rt(R), rt(R)

        m2 = carver(REG2, REG3)
        xg = m2(KT, 2 * SL)
        y_pair = m2(D)
        hid = [m2(FT, SL) for _ in range(2)]
        silu_s = m2(FT, SL)
        gu_s = [m2(FE) for _ in range(2)]

        s_h, s_par, s_vec, s_router = sem("h_loaded"), sem("b_loaded"), sem("vectors_loaded"), sem("router_loaded")
        s_cpar, s_uout, s_yout = sem("c_loaded"), sem("u_in_dram"), sem("y_in_dram")
        ring = [sem(f"ring_full{i}") for i in range(8)]
        s_const, s_rep0, s_t0, s_x0, s_stat = (sem("constants_ready"), sem("b_rep_cleared"), sem("t_cleared"),
                                               sem("x_prev_cleared"), sem("stat_set"))
        s_pool, s_dve, s_root = sem("pool_step"), sem("vector_step"), sem("root_ready")
        s_sq, s_rs, s_diag = sem("squares_summed"), sem("mean_inverse_ready"), sem("diag_ready")
        s_hps, s_hev, s_gev = sem("h_transposed"), sem("h_copied"), sem("hs_copied")
        s_ang, s_trig, s_n4, s_n4t, s_rho, s_pow = (sem("angle_ready"), sem("trig_ready"), sem("nat4_ready"),
                                                    sem("nat4_transposed"), sem("nat4_copied"), sem("powers_ready"))
        s_bc, s_bct, s_bce, s_bcv = (sem("stacks_ready"), sem("stacks_transposed"), sem("stacks_copied_even"),
                                     sem("stacks_copied_odd"))
        s_u, s_uev, s_uch, s_du = sem("u_done"), sem("u_copied"), sem("u_shuffled"), sem("du_ready")
        s_wt, s_w, s_gp, s_g, s_gt, s_gte, s_rep = (sem("w_step"), sem("w_ready"), sem("g_step"), sem("g_ready"),
                                                    sem("g_transposed"), sem("g_copied"), sem("b_rep_ready"))
        s_tp, s_fr, s_sn, s_tab = (sem("table_step"), sem("phase_ready"), sem("sine_step"),
                                         sem("tables_ready"))
        s_s, s_sev, s_qs, s_ch, s_zz, s_qz, s_xp = (sem("s_done"), sem("s_copied"), sem("s_turned"), sem("chain_step"),
                                                    sem("scan_done"), sem("z_turned"), sem("x_prev_ready"))
        s_t, s_tev, s_y, s_yev, s_ych, s_z = (sem("t_done"), sem("t_copied"), sem("y_done"), sem("y_copied"),
                                              sem("y_shuffled"), sem("y_ready"))
        s_gelu, s_glu, s_sig, s_gl, s_new, s_res = (sem("gelu_done"), sem("glu_done"), sem("gate_ready"),
                                                    sem("gated_ready"), sem("h_new_ready"), sem("residual_written"))
        s_nps, s_nev, s_log, s_gw, s_ssz, s_ssp = (sem("h_new_transposed"), sem("h_new_natural"), sem("logits_added"),
                                                   sem("router_scaled"), sem("partial_cleared"), sem("partial_squares"))
        s_tri, s_mask, s_rank, s_xn, s_count, s_rt, s_ex = (
            sem("triangle_ready"), sem("mask_ready"), sem("rank_done"), sem("xn_ready"), sem("count_ready"),
            sem("exponents_ready"), sem("exponentials_ready"))
        s_pick, s_pgt, s_pgte, s_gath, s_xg = (sem("pick_ready"), sem("pick_transposed"),
                                                       sem("pick_copied"), sem("gathered"), sem("xg_copied"))
        s_gu, s_guc, s_gut, s_silu, s_hid = (sem("gate_up_done"), sem("gate_up_copied"), sem("gate_up_transposed"),
                                             sem("silu_done"), sem("hidden_ready"))
        s_yp, s_ye, s_sc, s_acc = sem("down_done"), sem("down_copied"), sem("scattered"), sem("added")
        s_moe, s_fps, s_fev, s_fsq, s_gf, s_o, s_out = (sem("moe_over"), sem("final_transposed"), sem("final_copied"),
                                                        sem("final_squares"), sem("g_final_loaded"),
                                                        sem("out_ready"), sem("out_stored"))

        def need(eng, s, n):
            if not (isinstance(n, int) and n <= 0):
                eng.wait_ge(s, n)

        def runs(eng, n, body, last):
            body(0)
            with eng.Fori(1, n - last) as it:
                body(it)
            if last:
                body(n - 1)

        u_dram = [nc.dram_tensor(f"u_dram{i}", (P, T), F32).ap() for i in range(2)]
        y_dram = [nc.dram_tensor(f"y_dram{i}", (P, T), F32).ap() for i in range(2)]
        x_steps = a["x"].rearrange("b (c s) d -> (b s) c d", s=L)
        meta_steps = a["meta_tokens"].rearrange("(c s) d -> s c d", s=L)
        w_in = a["s5_w_in"].rearrange("a (k p) (n w) -> p (a n) k w", p=P, w=256)
        w_glu = a["s5_w_glu"].rearrange("a (k p) (n w) -> p (a n) k w", p=P, w=256)
        w_gu = [a[n].rearrange("a e (i k p) f -> p (a e i) k f", p=P, i=2) for n in ("moe_w_gate", "moe_w_up")]
        w_dn = a["moe_w_down"].rearrange("a e (i f p) d -> p (a e i) f d", p=P, i=2)
        out_steps = out.rearrange("b (c s) d -> (b s) c d", s=L)

        def in_slot(i):
            return slot[i].rearrange("p (k w) -> p k w", k=KT)

        def gu_slot(i):
            return slot[i].rearrange("p (k f) -> p k f", k=KT // 2)

        def dn_slot(i):
            return slot[i].rearrange("p (f d) -> p f d", f=2)

        def one(v, m):
            v = v[:, bass.ds(m, 1)]
            names = " ".join("abcd"[:v.ndim - 2])
            return v.rearrange(f"p x {names} -> p (x {names[0]}) {names[1:]}".rstrip())

        def flat(v):
            return v.rearrange("p g c -> p (g c)")

        g_final = slot[0][0:R, 0:D]
        f_out = at(RING + UNIT, 3, D)

        BEFORE = [8, 8, 4, 4, 0, 0, 0, 0]

        block = ctx.enter_context(nc.Block())

        @block.sync
        def _(sp):
            for s in range(L):
                t, r0 = s // 3, (s % 3) * C
                sp.dma_start(h_nat[r0:r0 + MC, t, :], meta_steps[s]).then_inc(s_h, 16)
                sp.dma_start(h_nat[r0 + MC:r0 + C, t, :], x_steps[s]).then_inc(s_h, 16)
            for n in range(2):
                sp.dma_start(in_slot(n), w_in[:, n]).then_inc(ring[n], 16)

            def u_shuffle(m, j):
                sp.wait_ge(s_uev, m + 1)
                sp.dma_start(u_dram[j % 2], u_sb[j % 2]).then_inc(s_uout, 16)
                sp.wait_ge(s_uout, (m + 1) * 16)
                for s in range(L):
                    q = L - 1 - s
                    sp.dma_start(u_ch[j % 4][H * q:H * q + H],
                                 u_dram[j % 2].rearrange("(g h) (s c) -> s h g c", g=GT, s=L)[s]
                                 ).then_inc(s_uch, 16)

            def y_shuffle(m, j):
                sp.wait_ge(s_yev, m + 1)
                sp.dma_start(y_dram[j % 2], flat(y_sb)).then_inc(s_yout, 16)
                sp.wait_ge(s_yout, (m + 1) * 16)
                for g in range(GT):
                    sp.dma_start(y_ch[j % 2][H * g:H * g + H].rearrange("h (t c) -> h t c", t=L),
                                 y_dram[j % 2].rearrange("(t h) (g c) -> g h t c", t=L, g=GT)[g]
                                 ).then_inc(s_ych, 16)

            u_shuffle(0, 0)
            u_shuffle(1, 1)

            def tiles(it):
                last = isinstance(it, int) and it == 3
                for j in range(4):
                    m = it * 4 + j
                    if j % 2 == 0 and not last:
                        unit = sp.snap(it * 2 + (j // 2 + 2))
                        sp.wait_ge(s_u, m + 2)
                        sp.dma_start(in_slot(j // 2), one(w_in, unit)).then_inc(ring[j // 2], 16)
                    if not (last and j >= 2):
                        u_shuffle(m + 2, j + 2)
                    if last and j == 1:
                        sp.wait_ge(s_u, KT)
                        for i in range(2):
                            sp.dma_start(in_slot(i), w_glu[:, 8 * i]).then_inc(ring[i], 16)
                    y_shuffle(m, j)

            runs(sp, 4, tiles, 1)
            sp.wait_ge(s_z, KT)
            for i in range(2):
                sp.dma_start(in_slot(2 + i), w_glu[:, 1 + 8 * i]).then_inc(ring[2 + i], 16)
            sp.dma_start(w_router[:, :, 0:EG], a["moe_w_coarse"].rearrange("a (k p) e -> p (a k) e", p=P)
                         ).then_inc(s_router, 16)
            sp.dma_start(w_router[:, :, EG:], a["moe_w_fine"].rearrange("a (k p) e -> p (a k) e", p=P)
                         ).then_inc(s_router, 16)
            sp.dma_start(b_router[:, 0:EG], a["moe_b_coarse"].to_broadcast((P, EG))).then_inc(s_router, 16)
            sp.dma_start(b_router[:, EG:], a["moe_b_fine"].to_broadcast((P, E))).then_inc(s_router, 16)

            def expert_stage(q, g, s2):
                if g < 4:
                    unit = sp.snap(q * 4 + g) if not isinstance(q, int) else q * 4 + g
                    sp.dma_start(gu_slot(s2), one(w_gu[0], unit)).then_inc(ring[s2], 16)
                    sp.dma_start(gu_slot(s2 + 1), one(w_gu[1], unit)).then_inc(ring[s2 + 1], 16)
                else:
                    for x in range(2):
                        sp.dma_start(dn_slot(s2 + x), one(w_dn, q * 4 + (2 * x + g - 4))).then_inc(ring[s2 + x], 16)

            def glu_pairs(it):
                for b in range(2):
                    unit = sp.snap(it * 2 + (b + 2))
                    sp.wait_ge(s_glu, it * 4 + (2 * b + 2))
                    sp.dma_start(in_slot(2 * b), one(w_glu, unit)).then_inc(ring[2 * b], 16)
                    sp.dma_start(in_slot(2 * b + 1), one(w_glu, unit + 8)).then_inc(ring[2 * b + 1], 16)

            glu_pairs(0)
            expert_stage(0, 2, 4)
            expert_stage(0, 3, 6)
            with sp.Fori(1, 3) as it:
                glu_pairs(it)
            sp.wait_ge(s_glu, 14)
            expert_stage(0, 0, 0)
            sp.wait_ge(s_glu, 16)
            expert_stage(0, 1, 2)

            def slots_used(q, g):
                if g < 4:
                    sp.wait_ge(s_gu, q * 4 + (g + 1))
                else:
                    sp.wait_ge(s_yp, q * 4 + 4)

            def expert_pass(r):
                if not isinstance(r, int):
                    for n in range(4):
                        slots_used(r * NPAIR - 1, n + 2)
                        expert_stage(0, n, 2 * n)
                with sp.Fori(0, NPAIR // 2 - 1) as it:
                    for n in range(12):
                        slots_used(r * NPAIR + it * 2 + n // 6, n % 6)
                        expert_stage(it * 2 + (n + 4) // 6, (n + 4) % 6, 2 * (n % 4))
                for n in range(6 * NPAIR - 8, 6 * NPAIR):
                    slots_used(r * NPAIR + (n - 4) // 6, (n - 4) % 6)
                    expert_stage(n // 6, n % 6, 2 * (n % 4))

            def load_g_final(passes):
                sp.wait_ge(s_yp, passes * (NPAIR * 4))
                sp.dma_start(g_final, a["norm_final"].rearrange("(a d) -> a d", a=1).to_broadcast((R, D))
                             ).then_inc(s_gf, 16)

            expert_pass(0)
            sp.wait_ge(s_count, 1)
            most = sp.value_load(count_sb[0:1, 0:1], min_val=0, max_val=T)
            with sp.If(most > SL):
                with sp.Fori(1, NPASS) as r:
                    expert_pass(r)
                load_g_final(NPASS)
            with sp.Else():
                load_g_final(1)
            for s in range(L):
                t, r0 = s // 3, (s % 3) * C
                sp.wait_ge(s_o, t + 1)
                sp.dma_start(out_steps[s], f_out[r0 + MC:r0 + C, t, :]).then_inc(s_out, 16)
            sp.wait_ge(s_out, 16 * L)

        @block.gpsimd
        def _(pool):
            steps = [0]

            def step(ins):
                steps[0] += 1
                ins.then_inc(s_pool, 1)
                pool.wait_ge(s_pool, steps[0])

            pool.dma_start(c_nat[:, :, 0, :], a["s5_c_re"].rearrange("a g h n -> (a g) h n")).then_inc(s_cpar, 16)
            pool.dma_start(c_nat[:, :, 1, :], a["s5_c_im"].rearrange("a g h n -> (a g) h n")).then_inc(s_cpar, 16)
            step(pool.memset(ident, 0.0))
            step(pool.affine_select(out=ident, in_=ident, compare_op=ALU.not_equal, fill=1.0, base=0,
                                    pattern=[[-1, P]], channel_multiplier=1))
            step(pool.memset(turn, 0.0))
            step(pool.affine_select(out=turn, in_=turn, compare_op=ALU.not_equal, fill=1.0, base=-NS,
                                    pattern=[[-1, P]], channel_multiplier=1))
            step(pool.affine_select(out=turn, in_=turn, compare_op=ALU.not_equal, fill=-1.0, base=NS,
                                    pattern=[[-1, P]], channel_multiplier=1))
            step(pool.iota(iota, pattern=[[1, SL]], base=0, channel_multiplier=0,
                           allow_small_or_imprecise_dtypes=True))
            step(pool.tensor_scalar(notfirst, iota[:, 0:C], 1.0, None, ALU.min))
            pool.memset(x_prev, 0.0).then_inc(s_x0, 1)
            pool.memset(stat, 1.0).then_inc(s_stat, 1)
            step(pool.memset(round_c, ROUND))
            step(pool.memset(quarter, math.pi / 2))
            pool.iota(iota, pattern=[[1, SL]], base=0, channel_multiplier=0,
                      allow_small_or_imprecise_dtypes=True).then_inc(s_const, 1)

            def tables(m, j):
                ph = phi8[:, bass.ds(m * GT, GT)].unsqueeze(2).broadcast_to((P, GT, C))
                rh = rho8[:, bass.ds(m * GT, GT)].unsqueeze(2).broadcast_to((P, GT, C))
                io = iota[:, 0:C].unsqueeze(1).broadcast_to((P, GT, C))
                nf = notfirst.unsqueeze(1).broadcast_to((P, GT, C))
                rc = round_c.unsqueeze(2).broadcast_to((P, GT, C))
                need(pool, s_tab, m)
                need(pool, s_xp, m - 1)
                pool.tensor_tensor(frac, ph, io, ALU.mult).then_inc(s_tp, 1)
                pool.wait_ge(s_tp, m * 4 + 1)
                pool.tensor_tensor(whole, frac, rc, ALU.add).then_inc(s_tp, 1)
                pool.wait_ge(s_tp, m * 4 + 2)
                pool.tensor_tensor(whole, whole, rc, ALU.subtract).then_inc(s_tp, 1)
                pool.wait_ge(s_tp, m * 4 + 3)
                pool.tensor_tensor(frac, frac, whole, ALU.subtract).then_inc(s_fr, 1)
                pool.tensor_tensor(mag_t[j % 2], rh, nf, ALU.mult).then_inc(s_tp, 1)

            def g_of(m):
                full = (P, GT, L, H)
                g0 = bass.ds(m * GT, GT)
                pr = pow_re[:, 0:L, g0].rearrange("p q g -> p g q").unsqueeze(3).broadcast_to(full)
                pi = pow_im[:, 0:L, g0].rearrange("p q g -> p g q").unsqueeze(3).broadcast_to(full)
                v1 = b1[:, :, g0].rearrange("p h g -> p g h").unsqueeze(2).broadcast_to(full)
                v2 = b2[:, :, g0].rearrange("p h g -> p g h").unsqueeze(2).broadcast_to(full)
                need(pool, s_g, m)
                pool.tensor_tensor(g_tmp, v2, pi, ALU.mult).then_inc(s_gp, 1)
                need(pool, s_gt, m)
                pool.tensor_tensor(g_sb, v1, pr, ALU.mult).then_inc(s_gp, 1)
                pool.wait_ge(s_gp, m * 2 + 2)
                pool.tensor_tensor(g_sb, g_sb, g_tmp, ALU.add).then_inc(s_g, 1)

            def rep_of(m):
                pool.wait_ge(s_rep0, 1)
                need(pool, s_t, m)
                v = b1[:, :, bass.ds(m * GT, GT)].rearrange("p h g -> p g h").unsqueeze(2)
                pool.tensor_copy(b_rep[:, :, 0:L + 1:2, :], v.broadcast_to((P, GT, L // 2 + 1, H))).then_inc(s_rep, 1)

            pool.wait_ge(s_rho, 4)
            tables(0, 0)
            pool.wait_ge(s_bct, 16)
            pool.memset(b_rep, 0.0).then_inc(s_rep0, 1)
            pool.memset(t_sb, 0.0).then_inc(s_t0, 1)
            pool.wait_ge(s_rep0, 1)
            pool.wait_ge(s_bce, 8)
            pool.wait_ge(s_bcv, 8)
            pool.wait_ge(s_pow, 1)
            g_of(0)
            rep_of(0)

            def tiles(it):
                for j in range(4):
                    m = it * 4 + j
                    if isinstance(m, int) and m == 0:
                        continue
                    tables(m, j)
                    g_of(m)
                    rep_of(m)

            runs(pool, 4, tiles, 0)

            def residuals(it):
                for j in range(4):
                    m = it * 4 + j
                    pool.wait_ge(s_const, 1)
                    pool.wait_ge(s_new, m + 1)
                    pool.tensor_copy(one_res(m), h_new[j % 2]).then_inc(s_res, 1)

            def one_res(m):
                return hT[:, bass.ds(m, 1), :].rearrange("p a t -> p (a t)")

            runs(pool, 4, residuals, 0)
            pool.wait_ge(s_glu, KT)
            step(pool.memset(ones, 1.0))
            pool.affine_select(out=before, in_=ones, compare_op=ALU.is_gt, fill=0.0, base=0,
                               pattern=[[1, R]], channel_multiplier=-1).then_inc(s_tri, 1)

        @block.scalar
        def _(act):
            act.dma_start(small[0], a["s5_a_re"].rearrange("a g n -> (a g) n")).then_inc(s_vec, 16)
            act.dma_start(small[1], a["s5_a_im"].rearrange("a g n -> (a g) n")).then_inc(s_vec, 16)
            with nc.allow_non_contiguous_dma(reason="small vectors, one element per partition and tile"):
                act.dma_start(small[2][:, 0:1], a["s5_log_dt"].rearrange("a g -> g a")).then_inc(s_vec, 16)
                act.dma_start(g_mix, a["norm_mix"].rearrange("a (k p) -> p (a k)", p=P)).then_inc(s_vec, 16)
                act.dma_start(g_ffn, a["norm_ffn"].rearrange("a (k p) -> p (a k)", p=P)).then_inc(s_vec, 16)
                act.dma_start(d_skip, a["s5_d"].rearrange("a (k p) -> p (a k)", p=P)).then_inc(s_vec, 16)
            act.dma_start(b_raw[:, 0], a["s5_b_re"].rearrange("a g n h -> (a g) n h")).then_inc(s_par, 16)
            act.dma_start(b_raw[:, 1], a["s5_b_im"].rearrange("a g n h -> (a g) n h")).then_inc(s_par, 16)

            act.wait_ge(s_h, 16 * 2 * L)
            act.wait_ge(s_stat, 1)
            for t in range(3):
                junk = hsT.rearrange("p k t -> p (k t)")[0:TR[t], 0:D]
                act.activation(junk, h_nat[0:TR[t], t, :], ACT.Square,
                               accum_out=stat3[0][0:TR[t], t:t + 1]).then_inc(s_sq, 1)
                act.wait_ge(s_sq, t + 1)
            act.wait_ge(s_rs, 1)
            act.activation(stat3[2], stat3[1], ACT.Sqrt).then_inc(s_root, 1)

            act.wait_ge(s_vec, 16 * 6)
            for k in range(KT):
                act.wait_ge(s_hps, 2 * k + 2)
                act.activation(hsT[:, k, :], bank[(2 * k + 1) % 4][:, 0:T], ACT.Copy,
                               scale=g_mix[:, k:k + 1]).then_inc(s_gev, 1)

            def u_copy(m, j):
                act.wait_ge(s_u, m + 1)
                need(act, s_uout, (m - 1) * 16)
                need(act, s_du, m - 1)
                act.activation(u_sb[j % 2], bank[j % 2][:, 0:T], ACT.Copy).then_inc(s_uev, 1)

            def gt_copy(m):
                act.wait_ge(s_gt, m + 1)
                need(act, s_s, m)
                for i in range(2):
                    act.activation(gt_sb[:, 4 * i:4 * i + 4, :], bank[4 + i][:, :].rearrange("p (g n) -> p g n", g=4),
                                   ACT.Copy).then_inc(s_gte, 1)

            def sines(m, j):
                act.wait_ge(s_fr, m + 1)
                need(act, s_xp, m - 1)
                act.activation(sin_t[j % 2], frac, ACT.Sin, scale=TWO_PI).then_inc(s_sn, 1)
                act.activation(cos_t[j % 2], frac, ACT.Abs).then_inc(s_sn, 1)
                act.wait_ge(s_sn, m * 2 + 2)
                act.activation(cos_t[j % 2], cos_t[j % 2], ACT.Sin, bias=quarter, scale=-TWO_PI).then_inc(s_tab, 1)

            act.wait_ge(s_ang, 1)
            act.activation(small[5], small[4], ACT.Sin, scale=TWO_PI).then_inc(s_trig, 1)
            act.activation(small[6], small[4], ACT.Sin, scale=TWO_PI / 2).then_inc(s_trig, 1)
            u_copy(0, 0)
            u_copy(1, 1)
            for i in range(0, 16, 2):
                act.wait_ge(s_bct, i + 1)
                dst = (b1, b2, c1, c2)[i // 4][:, 4 * (i % 4):4 * (i % 4) + 4, :]
                act.activation(dst, bank[2 + i % 4][:, :].rearrange("p (h g) -> p h g", h=4), ACT.Copy
                               ).then_inc(s_bce, 1)
            sines(0, 0)
            gt_copy(0)

            def tiles(it):
                last = isinstance(it, int) and it == 3
                for j in range(4):
                    m = it * 4 + j
                    act.wait_ge(s_s, m + 1)
                    act.activation(flat(s_sb), bank[6][:, 0:GT * C], ACT.Copy).then_inc(s_sev, 1)
                    act.wait_ge(s_t, m + 1)
                    if isinstance(m, int) and m == 0:
                        act.wait_ge(s_t0, 1)
                    for i in range(4):
                        n = 2 + 2 * i
                        for b in range(2):
                            act.activation(t_sb[32 * i:32 * i + 32, 4 * b:4 * b + 4, L - n:L, :],
                                           bank[2 + b][32 * i:32 * i + 32, :].rearrange(
                                               "p (g v h) -> p g v h", g=4, v=L)[:, :, 0:n, :],
                                           ACT.Copy).then_inc(s_tev, 1)
                    if not (last and j == 3):
                        sines(m + 1, j + 1)
                    if not (last and j >= 2):
                        u_copy(m + 2, j)
                    if not (last and j == 3):
                        gt_copy(m + 1)
                    act.wait_ge(s_y, m + 1)
                    need(act, s_yout, m * 16)
                    act.activation(flat(y_sb), bank[7][:, 0:GT * C], ACT.Copy).then_inc(s_yev, 1)

            runs(act, 4, tiles, 1)

            for i in range(4):
                act.wait_ge(s_z, 4 * i + 4)
                act.activation(zT[:, 4 * i:4 * i + 4, :], zT[:, 4 * i:4 * i + 4, :], ACT.Gelu_apprx_tanh
                               ).then_inc(s_gelu, 1)

            def squares(m):
                act.wait_ge(s_nev, m * 2 + 2)
                for t in range(3):
                    need(act, s_ssp, m * 3 + t)
                    act.activation(square_s[0:TR[t], :], xn[0:TR[t], t, bass.ds(m * P, P)], ACT.Square,
                                   accum_out=sumsq[0:TR[t], t, bass.ds(m, 1)]).then_inc(s_ssp, 1)

            def glu_tiles(it):
                for j in range(4):
                    m = it * 4 + j
                    act.wait_ge(s_glu, m + 1)
                    need(act, s_gl, m - 1)
                    act.activation(gate_s[j % 2], bank[2 * (j % 2) + 1][:, 0:T], ACT.Sigmoid).then_inc(s_sig, 1)
                    if isinstance(m, int) and m == 0:
                        act.wait_ge(s_ssz, 1)
                    else:
                        squares(m - 1)

            runs(act, 4, glu_tiles, 0)
            squares(KT - 1)

            act.wait_ge(s_rs, 2)
            act.activation(stat3[2], stat3[1], ACT.Sqrt).then_inc(s_root, 1)
            act.wait_ge(s_rt, 1)
            act.activation(ex4[0:R], ex4[0:R], ACT.Exp).then_inc(s_ex, 1)
            act.wait_ge(s_rt, 2)
            act.activation(col[3][0:R], col[3][0:R], ACT.Exp).then_inc(s_ex, 1)

            def expert_pass(r):
                def experts(it):
                    for j in range(4):
                        e = r * E + (it * 4 + j)
                        q = r * NPAIR + (it * 2 + j // 2)
                        act.wait_ge(s_gu, e * 2 + 2)
                        act.activation(gu_s[j % 2], bank[j % 2][:, :], ACT.Copy).then_inc(s_guc, 1)
                        act.wait_ge(s_gut, e + 1)
                        need(act, s_hid, e)
                        act.activation(silu_s, bank[2][:, :].rearrange("p (f s) -> p f s", f=FT)[:, :, 0:SL],
                                       ACT.Silu).then_inc(s_silu, 1)
                        if j % 2 == 1:
                            for c in range(4):
                                act.wait_ge(s_yp, q * 4 + (c + 1))
                                act.activation(y_pair[:, 512 * c:512 * c + 512], bank[4 + c % 2][:, :],
                                               ACT.Copy).then_inc(s_ye, 1)

                runs(act, E // 4, experts, 0)

            expert_pass(0)
            act.wait_ge(s_count, 1)
            most = act.value_load(count_sb[0:1, 0:1], min_val=0, max_val=T)
            with act.If(most > SL):
                with act.Fori(1, NPASS) as r:
                    expert_pass(r)

            for t in range(3):
                act.wait_ge(s_fev, 4 * t + 4)
                act.activation(f_out[0:TR[t], t, :], xn[0:TR[t], t, :], ACT.Square,
                               accum_out=stat3[0][0:TR[t], t:t + 1]).then_inc(s_fsq, 1)
            act.wait_ge(s_rs, 3)
            act.activation(stat3[2], stat3[1], ACT.Sqrt).then_inc(s_root, 1)

        @block.tensor
        def _(pe):
            pe.wait_ge(s_const, 1)
            pe.wait_ge(s_h, 16 * 2 * L)
            pe.wait_ge(s_diag, 3)
            for k in range(KT):
                for scaled in range(2):
                    n = 2 * k + scaled
                    need(pe, s_gev if scaled else s_hev, k - 1)
                    for t in range(3):
                        rows = TR[t]
                        src = h_nat[0:rows, t, P * k:P * k + P]
                        dst = bank[n % 4][:, TO[t]:TO[t] + rows]
                        if scaled:
                            last = pe.matmul(dst, src, diag[0:rows, t, 0:rows], start=True, stop=True)
                        else:
                            last = pe.transpose(dst, src, ident[0:rows, 0:rows])
                    last.then_inc(s_hps, 1)

            def u_product(m, j, s2, n):
                pe.wait_ge(ring[s2], n * 16)
                need(pe, s_uev, m - 1)
                for k in range(KT):
                    last = pe.matmul(bank[j % 2][:, 0:T], in_slot(s2)[:, k, P * (j % 2):P * (j % 2) + P],
                                     hsT[:, k, :], start=(k == 0), stop=(k == KT - 1))
                last.then_inc(s_u, 1)

            def g_transpose(m):
                pe.wait_ge(s_g, m + 1)
                need(pe, s_gte, m * 2)
                for g in range(GT):
                    last = pe.transpose(bank[4 + g // 4][:, P * (g % 4):P * (g % 4) + P],
                                        g_sb[:, g].rearrange("p q h -> p (q h)"), ident)
                last.then_inc(s_gt, 1)

            pe.wait_ge(s_gev, KT)
            pe.wait_ge(s_hev, KT)
            u_product(0, 0, 0, 1)
            u_product(1, 1, 0, 1)
            pe.wait_ge(s_n4, 4)
            for i in range(4):
                last = pe.transpose(bank[6][:, P * i:P * i + P], nat4[:, i].rearrange("p a n -> p (a n)"), ident)
            last.then_inc(s_n4t, 1)
            bn = b_nat.rearrange("p s n h -> p (s n) h")
            pe.wait_ge(s_bc, 1)
            for i in range(16):
                need(pe, s_bce if i % 2 == 0 else s_bcv, i // 2 - 1)
                for x in range(4):
                    h = 4 * (i % 4) + x
                    src = (bn[:, NS:3 * NS, h], bn[:, 0:2 * NS, h],
                           c_nat[:, h, 0:2, :].rearrange("p s n -> p (s n)"),
                           c_nat[:, h, 1:3, :].rearrange("p s n -> p (s n)"))[i // 4]
                    last = pe.transpose(bank[2 + i % 4][:, P * x:P * x + P], src, ident)
                last.then_inc(s_bct, 1)
            pe.wait_ge(s_bce, 8)
            pe.wait_ge(s_bcv, 8)
            pe.wait_ge(s_rho, 4)
            g_transpose(0)

            def tiles(it):
                last_it = isinstance(it, int) and it == 3
                for j in range(4):
                    m = it * 4 + j
                    w = w_sb[j % 2]
                    pe.wait_ge(s_uch, (m + 1) * (16 * L))
                    pe.wait_ge(s_gte, m * 2 + 2)
                    need(pe, s_xp, m)
                    for g in range(GT):
                        last = pe.matmul(bank[6][:, C * g:C * g + C], gt_sb[:, g], u_ch[j][:, g],
                                         start=True, stop=True)
                    last.then_inc(s_s, 1)
                    pe.wait_ge(s_w, m + 1)
                    pe.wait_ge(s_rep, m + 1)
                    need(pe, s_tev, m * 8)
                    for g in range(GT):
                        dst = bank[2 + g // 4][:, P * (g % 4):P * (g % 4) + P]
                        rep = b_rep[:, g].rearrange("p q h -> p (q h)")
                        pe.matmul(dst, rep[:, H:H + P], w[:, g, 0:L, :].rearrange("p q h -> p (q h)"),
                                  start=True, stop=False, skip_group_check=True)
                        last = pe.matmul(dst[:, H:P], rep[:, 0:P], w[:, g, 0:L - 1, :].rearrange("p q h -> p (q h)"),
                                         start=False, stop=True, skip_group_check=True)
                    last.then_inc(s_t, 1)
                    pe.wait_ge(s_sev, m + 1)
                    pe.matmul(bank[6][:, 0:GT * C], turn, flat(s_sb), start=True, stop=True).then_inc(s_qs, 1)
                    if not (last_it and j >= 2):
                        u_product(m + 2, j, ((j + 2) // 2) % 2, it + ((j + 2) // 4 + 1))
                    pe.wait_ge(s_zz, m + 1)
                    pe.matmul(bank[6][:, 0:GT * C], turn, flat(zz), start=True, stop=True).then_inc(s_qz, 1)
                    if not (last_it and j == 3):
                        g_transpose(m + 1)
                    pe.wait_ge(s_tev, m * 8 + 8)
                    pe.wait_ge(s_xp, m + 1)
                    need(pe, s_yev, m)
                    for g in range(GT):
                        dst = bank[7][:, C * g:C * g + C]
                        pe.matmul(dst, t_sb[:, g].rearrange("p t h -> p (t h)"), u_ch[j][:, g],
                                  start=True, stop=False)
                        last = pe.matmul(dst, w[:, g, 1:L + 1, :].rearrange("p t h -> p (t h)"),
                                         x_prev[:, g, 0:C], start=False, stop=True)
                    last.then_inc(s_y, 1)

            runs(pe, 4, tiles, 1)

            def new_rows(m, j):
                first = isinstance(m, int) and m == 0
                pe.wait_ge(s_new, m + 1)
                need(pe, s_nev, (m - 1) * 2)
                for t in range(3):
                    last = pe.transpose(bank[4 + j % 2][0:TR[t], P * t:P * t + P], h_new[j % 2][:, TO[t]:TO[t] + TR[t]],
                                        ident)
                last.then_inc(s_nps, 1)
                if first:
                    pe.wait_ge(s_gw, 1)
                wr = w_router[:, bass.ds(m, 1), :].rearrange("p a e -> p (a e)")
                for t in range(3):
                    last = pe.matmul(bank[6][0:TR[t], 64 * t:64 * t + EG + E], h_new[j % 2][:, TO[t]:TO[t] + TR[t]],
                                     wr, start=(first and t == 0), stop=(t == 2), skip_group_check=True)
                last.then_inc(s_log, 1)

            def glu_tiles(it):
                for j in range(4):
                    m = it * 4 + j
                    s2 = 2 * (j // 2)
                    need(pe, s_new, m - 1)
                    for half in range(2):
                        pe.wait_ge(ring[s2 + half], (it + (BEFORE[s2] - 4 + 1)) * 16)
                        for k in range(KT):
                            if half == 0 and k % 4 == 0 and isinstance(m, int) and m == 0:
                                pe.wait_ge(s_gelu, k // 4 + 1)
                            last = pe.matmul(bank[2 * (j % 2) + half][:, 0:T],
                                             in_slot(s2 + half)[:, k, P * (j % 2):P * (j % 2) + P], zT[:, k, :],
                                             start=(k == 0), stop=(k == KT - 1))
                    last.then_inc(s_glu, 1)
                    if not (isinstance(m, int) and m == 0):
                        new_rows(m - 1, j + 1)

            runs(pe, 4, glu_tiles, 0)
            new_rows(KT - 1, KT - 1)

            pe.wait_ge(s_tri, 1)
            pe.wait_ge(s_mask, 1)
            for t in range(3):
                for t0 in range(t + 1):
                    left = before if t0 == t else ones
                    last = pe.matmul(bank[7][0:TR[t], E * t:E * t + E], left[0:TR[t0], 0:TR[t]],
                                     hot[0][0:TR[t0], :, t0], start=(t0 == 0), stop=(t0 == t))
            for t0 in range(3):
                last = pe.matmul(bank[7][0:32, E * 3:E * 4], ones[0:TR[t0], 0:32], hot[0][0:TR[t0], :, t0],
                                 start=(t0 == 0), stop=(t0 == 2))
            last.then_inc(s_rank, 1)

            def gather(r, q, n, xs):
                for x in xs:
                    if x == 0:
                        pe.wait_ge(s_pick, n + 1)
                        need(pe, s_pgte, n)
                        for t in range(3):
                            last = pe.transpose(bank[3][:, TO[t]:TO[t] + TR[t]],
                                                pick_g[0:TR[t], t].rearrange("p a s -> p (a s)"),
                                                ident[0:TR[t], 0:TR[t]])
                        last.then_inc(s_pgt, 1)
                        need(pe, s_acc, (n - (0 if isinstance(q, int) and q == 0 else 1)) * KT)
                    if x >= 2:
                        pe.wait_ge(s_xg, n * 4 + (x - 1))
                    for k in range(4 * x, 4 * x + 4):
                        for t in range(3):
                            last = pe.matmul(bank[6 + x % 2][:, P * (k % 4):P * (k % 4) + P],
                                             xn[0:TR[t], t, P * k:P * k + P],
                                             pick[0:TR[t], t].rearrange("p a s -> p (a s)"),
                                             start=(t == 0), stop=(t == 2))
                    last.then_inc(s_gath, 1)

            def scatter(n, par):
                pe.wait_ge(s_pgte, n + 1)
                pe.wait_ge(s_ye, n * 4 + 4)
                for k in range(KT):
                    if k >= 2:
                        pe.wait_ge(s_acc, n * KT + (k - 1))
                    pe.matmul(bank[6 + k % 2][:, 0:T], y_pair[:, P * k:P * k + P], pick_t[par],
                              start=True, stop=True).then_inc(s_sc, 1)

            def expert_pass(r):
                gather(r, 0, r * NPAIR, range(4))

                def experts(it):
                    def full(stage, i):
                        u = 2 * stage + i
                        return ring[u % 8], (r * 24 + it * 3 + (BEFORE[u % 8] + u // 8 + 1)) * 16

                    def gate_up(j):
                        e = r * E + (it * 4 + j)
                        n = r * NPAIR + (it * 2 + j // 2)
                        pe.wait_ge(s_xg, n * 4 + 4)
                        need(pe, s_guc, e - 1)
                        for half in range(2):
                            g = 6 * (j // 2) + 2 * (j % 2) + half
                            for i in range(2):
                                pe.wait_ge(*full(g, i))
                            for k in range(KT // 2):
                                for i in range(2):
                                    last = pe.matmul(bank[j % 2][SL * i:SL * i + SL, :],
                                                     xg[:, KT // 2 * half + k, SL * (j % 2):SL * (j % 2) + SL],
                                                     gu_slot((2 * g + i) % 8)[:, k, :],
                                                     start=(half == 0 and k == 0), stop=(half == 1 and k == KT // 2 - 1))
                            last.then_inc(s_gu, 1)

                    def turn_gate_up(j):
                        e = r * E + (it * 4 + j)
                        pe.wait_ge(s_guc, e + 1)
                        need(pe, s_hid, e)
                        for f in range(FT):
                            last = pe.transpose(bank[2][:, P * f:P * f + P], gu_s[j % 2][:, P * f:P * f + P], ident)
                        last.then_inc(s_gut, 1)

                    def down(pr):
                        n = r * NPAIR + (it * 2 + pr)
                        pe.wait_ge(s_hid, n * 2 + 2)
                        for g in (6 * pr + 4, 6 * pr + 5):
                            for i in range(2):
                                pe.wait_ge(*full(g, i))
                        for c in range(4):
                            need(pe, s_ye, n * 4 + (c - 1))
                            for f in range(FT):
                                for i in range(2):
                                    u = 2 * (6 * pr + 4 + f // 2) + i
                                    last = pe.matmul(bank[4 + c % 2][SL * i:SL * i + SL, :], hid[i][:, f, :],
                                                     dn_slot(u % 8)[:, f % 2, 512 * c:512 * c + 512],
                                                     start=(f == 0), stop=(f == FT - 1))
                            last.then_inc(s_yp, 1)

                    for pr in range(2):
                        q = it * 2 + pr
                        n = r * NPAIR + q
                        gate_up(2 * pr)
                        if not (isinstance(q, int) and q == 0):
                            scatter(n - 1, 1 - pr)
                        turn_gate_up(2 * pr)
                        gate_up(2 * pr + 1)
                        if isinstance(q, int) and q == NPAIR - 1:
                            turn_gate_up(2 * pr + 1)
                        else:
                            gather(r, q + 1, n + 1, (0, 1))
                            turn_gate_up(2 * pr + 1)
                            gather(r, q + 1, n + 1, (2, 3))
                        down(pr)

                runs(pe, E // 4, experts, 1)
                scatter(r * NPAIR + (NPAIR - 1), 1)

            pe.wait_ge(s_xn, 3)
            expert_pass(0)
            pe.wait_ge(s_count, 1)
            most = pe.value_load(count_sb[0:1, 0:1], min_val=0, max_val=T)
            with pe.If(most > SL):
                with pe.Fori(1, NPASS) as r:
                    expert_pass(r)

            pe.wait_ge(s_moe, 1)
            for n in range(12):
                t, k0 = n // 4, 4 * (n % 4)
                need(pe, s_fev, n - 3)
                for k in range(k0, k0 + 4):
                    last = pe.transpose(bank[n % 4][0:TR[t], P * (k % 4):P * (k % 4) + P],
                                        hT[:, k, TO[t]:TO[t] + TR[t]], ident)
                last.then_inc(s_fps, 1)

        @block.vector
        def _(dve):
            steps = [0]

            def step(ins):
                steps[0] += 1
                ins.then_inc(s_dve, 1)
                dve.wait_ge(s_dve, steps[0])

            def tt(o, x, y, op):
                step(dve.tensor_tensor(o, x, y, op))

            def ts(o, x, s1, op0, s2=None, op1=None):
                if op1 is None:
                    step(dve.tensor_scalar(o, x, s1, None, op0))
                else:
                    step(dve.tensor_scalar(o, x, s1, s2, op0, op1))

            def stt(o, x, s, y, op0, op1):
                step(dve.scalar_tensor_tensor(out=o, in0=x, scalar=s, in1=y, op0=op0, op1=op1))

            ADD, SUB, MUL, EQ = ALU.add, ALU.subtract, ALU.mult, ALU.is_equal
            sum_sq, inverse, root, rs = stat3

            def rms(n):
                ts(rs, sum_sq, 1.0 / D, MUL, EPS, ADD)
                dve.reciprocal(inverse, rs).then_inc(s_rs, 1)
                dve.wait_ge(s_root, n)
                tt(rs, rs, root, MUL)
                tt(rs, rs, root, MUL)
                ts(rs, rs, -0.5, MUL, 1.5, ADD)
                tt(rs, rs, root, MUL)

            dve.wait_ge(s_stat, 1)
            dve.wait_ge(s_sq, 3)
            rms(1)
            dve.wait_ge(s_const, 1)
            for t in range(3):
                dve.tensor_scalar(diag[0:TR[t], t, 0:TR[t]], ident[0:TR[t], 0:TR[t]], rs[0:TR[t], t:t + 1], None,
                                  MUL).then_inc(s_diag, 1)
            for k in range(KT):
                dve.wait_ge(s_hps, 2 * k + 1)
                dve.tensor_copy(hT[:, k, :], bank[(2 * k) % 4][:, 0:T]).then_inc(s_hev, 1)

            dve.wait_ge(s_vec, 16 * 6)
            lr, li = small[0], small[1]
            log_dt, n_, r_, p_, two, dt = (small[2][:, i:i + 1] for i in range(6))
            ts(n_, log_dt, 1.0 / math.log(2.0), MUL, ROUND, ADD)
            ts(n_, n_, ROUND, SUB)
            ts(n_, n_, -126.0, ALU.max, 127.0, ALU.min)
            stt(r_, n_, -0.693359375, log_dt, MUL, ADD)
            stt(r_, n_, 2.12194440e-4, r_, MUL, ADD)
            ts(p_, r_, 1.0 / 5040, MUL, 1.0 / 720, ADD)
            for c in (1.0 / 120, 1.0 / 24, 1.0 / 6, 0.5, 1.0, 1.0):
                ts(p_, p_, r_, MUL, c, ADD)
            ts(two.bitcast(I32), n_, 127.0, ADD, 8388608.0, MUL)
            tt(dt, p_, two, MUL)
            whl, ang = small[3], small[4]
            ts(ang, li, dt, MUL, INV_2PI, MUL)
            ts(whl, ang, ROUND, ADD)
            ts(whl, whl, ROUND, SUB)
            dve.tensor_tensor(ang, ang, whl, SUB).then_inc(s_ang, 1)
            em, y_ = small[7], small[8]
            ts(y_, lr, dt, MUL, EXP_FLOOR, ALU.max)
            ts(y_, y_, 1.0 / 32, MUL)
            ts(em, y_, 1.0 / math.factorial(9), MUL)
            for k in range(8, 0, -1):
                stt(em, em, 1.0 / math.factorial(k), y_, ADD, MUL)
            for _k in range(5):
                stt(em, em, 2.0, em, ADD, MUL)
            sn, hf, cm, cs, mg = small[5], small[6], small[10], small[11], small[12]
            dve.wait_ge(s_trig, 2)
            stt(cm, hf, -2.0, hf, MUL, MUL)
            ts(cs, cm, 1.0, ADD)
            ts(mg, em, 1.0, ADD)
            ar, ai, nr, den, cr, ci, tmp = small[13], small[14], small[15], small[8], small[9], small[3], small[5]
            tt(ar, mg, cs, MUL)
            tt(ai, mg, sn, MUL)
            tt(nr, em, cs, MUL)
            tt(nr, nr, cm, ADD)
            tt(den, lr, lr, MUL)
            tt(tmp, li, li, MUL)
            tt(den, den, tmp, ADD)
            step(dve.reciprocal(den, den))
            tt(cr, nr, lr, MUL)
            tt(tmp, ai, li, MUL)
            tt(cr, cr, tmp, ADD)
            tt(cr, cr, den, MUL)
            tt(ci, ai, lr, MUL)
            tt(tmp, nr, li, MUL)
            tt(ci, ci, tmp, SUB)
            tt(ci, ci, den, MUL)
            for _k in range(3):
                tt(mg, mg, mg, MUL)
            ts(ang, ang, float(L), MUL)
            whl = small[6]
            ts(whl, ang, ROUND, ADD)
            ts(whl, whl, ROUND, SUB)
            tt(ang, ang, whl, SUB)
            for i, v in enumerate((ar, ai, mg, ang)):
                dve.tensor_copy(nat4[:, i], v.unsqueeze(1).broadcast_to((P, 2, NS))).then_inc(s_n4, 1)
            dve.wait_ge(s_par, 16 * 2)
            dve.wait_ge(s_cpar, 16 * 2)
            crb = cr.unsqueeze(2).broadcast_to((P, NS, H))
            cib = ci.unsqueeze(2).broadcast_to((P, NS, H))
            tt(b_nat[:, 0], b_raw[:, 1], cib, MUL)
            tt(b_nat[:, 1], b_raw[:, 0], crb, MUL)
            tt(b_nat[:, 1], b_nat[:, 1], b_nat[:, 0], SUB)
            tt(b_nat[:, 0], b_raw[:, 0], cib, MUL)
            tt(b_nat[:, 2], b_raw[:, 1], crb, MUL)
            tt(b_nat[:, 2], b_nat[:, 2], b_nat[:, 0], ADD)
            ts(b_nat[:, 0], b_nat[:, 2], -1.0, MUL)
            ts(c_nat[:, :, 1, :], c_nat[:, :, 1, :], -1.0, MUL)
            dve.tensor_scalar(c_nat[:, :, 2, :], c_nat[:, :, 0, :], -1.0, None, MUL).then_inc(s_bc, 1)

            dve.wait_ge(s_n4t, 1)
            for i, o in enumerate((pow_re[:, 1, :], pow_im[:, 1, :], rho8, phi8)):
                dve.tensor_copy(o, bank[6][:, P * i:P * i + P]).then_inc(s_rho, 1)
            dve.wait_ge(s_rho, 4)
            for base in (1, 2, 4):
                shape = (P, base, G)
                kr = pow_re[:, base:base + 1, :].broadcast_to(shape)
                ki = pow_im[:, base:base + 1, :].broadcast_to(shape)
                xr, xi = pow_re[:, 1:1 + base, :], pow_im[:, 1:1 + base, :]
                o_re, o_im = pow_re[:, base + 1:2 * base + 1, :], pow_im[:, base + 1:2 * base + 1, :]
                tm = p_tmp[:, 0:base, :]
                tt(o_re, kr, xr, MUL)
                tt(tm, ki, xi, MUL)
                tt(o_re, o_re, tm, SUB)
                tt(o_im, kr, xi, MUL)
                tt(tm, ki, xr, MUL)
                tt(o_im, o_im, tm, ADD)
            step(dve.memset(pow_re[:, 0, :], 1.0))
            dve.memset(pow_im[:, 0, :], 0.0).then_inc(s_pow, 1)
            for i in range(1, 16, 2):
                dve.wait_ge(s_bct, i + 1)
                dst = (b1, b2, c1, c2)[i // 4][:, 4 * (i % 4):4 * (i % 4) + 4, :]
                dve.tensor_copy(dst, bank[2 + i % 4][:, :].rearrange("p (h g) -> p h g", h=4)).then_inc(s_bcv, 1)
            dve.wait_ge(s_pow, 1)
            dve.wait_ge(s_bcv, 8)
            dve.wait_ge(s_bce, 8)

            def w_of(m, j):
                full = (P, GT, L + 1, H)
                g0 = bass.ds(m * GT, GT)
                pr = pow_re[:, :, g0].rearrange("p q g -> p g q").unsqueeze(3).broadcast_to(full)
                pi = pow_im[:, :, g0].rearrange("p q g -> p g q").unsqueeze(3).broadcast_to(full)
                v1 = c1[:, :, g0].rearrange("p h g -> p g h").unsqueeze(2).broadcast_to(full)
                v2 = c2[:, :, g0].rearrange("p h g -> p g h").unsqueeze(2).broadcast_to(full)
                dve.tensor_tensor(w_tmp, v2, pi, MUL).then_inc(s_wt, 1)
                need(dve, s_y, m - 1)
                dve.tensor_tensor(w_sb[j % 2], v1, pr, MUL).then_inc(s_wt, 1)
                dve.wait_ge(s_wt, m * 2 + 2)
                dve.tensor_tensor(w_sb[j % 2], w_sb[j % 2], w_tmp, ADD).then_inc(s_w, 1)

            def z_of(m):
                return zT[:, bass.ds(m, 1), :].rearrange("p a t -> p (a t)")

            def d_times_u(m, j):
                dve.wait_ge(s_uev, m + 1)
                dve.tensor_scalar(z_of(m), u_sb[j % 2], d_skip[:, bass.ds(m, 1)], None, MUL).then_inc(s_du, 1)

            def y_add(m, j):
                dve.wait_ge(s_ych, (m + 1) * (16 * GT))
                dve.wait_ge(s_du, m + 1)
                dve.tensor_tensor(z_of(m), z_of(m), y_ch[j % 2], ADD).then_inc(s_z, 1)

            def tiles(it):
                last = isinstance(it, int) and it == 3
                for j in range(4):
                    m = it * 4 + j
                    turned = bank[6][:, 0:GT * C]
                    cos_m, sin_m = flat(cos_t[j % 2]), flat(sin_t[j % 2])
                    dve.wait_ge(s_tab, m + 1)
                    dve.wait_ge(s_sev, m + 1)
                    dve.tensor_tensor(flat(t1), cos_m, flat(s_sb), MUL).then_inc(s_ch, 1)
                    dve.wait_ge(s_qs, m + 1)
                    dve.tensor_tensor(flat(t2), sin_m, turned, MUL).then_inc(s_ch, 1)
                    dve.wait_ge(s_ch, m * 5 + 2)
                    dve.tensor_tensor(flat(t1), flat(t1), flat(t2), ADD).then_inc(s_ch, 1)
                    dve.wait_ge(s_ch, m * 5 + 3)
                    dve.wait_ge(s_tp, m * 4 + 4)
                    dve.tensor_tensor_scan(flat(zz), flat(mag_t[j % 2]), flat(t1), 0.0, MUL, ADD).then_inc(s_zz, 1)
                    if not (last and j == 3):
                        w_of(m + 1, j + 1)
                    dve.wait_ge(s_zz, m + 1)
                    dve.tensor_tensor(flat(t1), cos_m, flat(zz), MUL).then_inc(s_ch, 1)
                    dve.wait_ge(s_qz, m + 1)
                    dve.tensor_tensor(flat(t2), sin_m, turned, MUL).then_inc(s_ch, 1)
                    dve.wait_ge(s_ch, m * 5 + 5)
                    if isinstance(m, int) and m == 0:
                        dve.wait_ge(s_x0, 1)
                    dve.tensor_tensor(x_prev[:, :, 1:C + 1], t1, t2, SUB).then_inc(s_xp, 1)
                    if not (last and j >= 2):
                        d_times_u(m + 2, j)
                    if not (isinstance(m, int) and m == 0):
                        y_add(m - 1, j + 1)

            d_times_u(0, 0)
            d_times_u(1, 1)
            w_of(0, 0)
            runs(dve, 4, tiles, 1)
            y_add(KT - 1, KT - 1)

            dve.memset(sumsq, 0.0).then_inc(s_ssz, 1)
            dve.wait_ge(s_router, 16 * 4)
            dve.tensor_tensor(w_router, w_router, g_ffn.unsqueeze(2).broadcast_to((P, KT, EG + E)), MUL
                              ).then_inc(s_gw, 1)

            def to_rows(m, j):
                dve.wait_ge(s_nps, m + 1)
                src = bank[4 + j % 2][:, 0:3 * P].rearrange("p (t c) -> p t c", t=3)
                cols = bass.ds(m * P, P)
                dve.tensor_copy(xn[0:R, 0:2, cols], src[0:R, 0:2, :]).then_inc(s_nev, 1)
                dve.tensor_copy(xn[0:TR[2], 2, cols], src[0:TR[2], 2, :]).then_inc(s_nev, 1)

            def glu_tiles(it):
                for j in range(4):
                    m = it * 4 + j
                    dve.wait_ge(s_sig, m + 1)
                    need(dve, s_new, m)
                    dve.tensor_tensor(value_s, bank[2 * (j % 2)][:, 0:T], gate_s[j % 2], MUL).then_inc(s_gl, 1)
                    dve.wait_ge(s_gl, m + 1)
                    need(dve, s_res, m - 1)
                    need(dve, s_log, m - 1)
                    dve.tensor_tensor(h_new[j % 2], value_s, hT[:, bass.ds(m, 1), :].rearrange("p a t -> p (a t)"),
                                      ADD).then_inc(s_new, 1)
                    if not (isinstance(m, int) and m == 0):
                        to_rows(m - 1, j + 1)

            runs(dve, 4, glu_tiles, 0)
            to_rows(KT - 1, KT - 1)

            dve.wait_ge(s_ssp, 3 * KT)
            step(dve.tensor_reduce(sum_sq, sumsq[0:R], AX.X, ADD))
            rms(2)
            dve.wait_ge(s_nev, 2 * KT)
            dve.wait_ge(s_log, KT)
            step(dve.memset(logit, 0.0))
            step(dve.memset(coarse, -3.0e38))
            for t in range(3):
                rows = slice(0, TR[t])
                stt(logit[rows, t, :], bank[6][rows, 64 * t:64 * t + EG + E], rs[rows, t:t + 1], b_router[rows, :],
                    MUL, ADD)
            rows = slice(0, R)
            three = lambda v, n: v[rows].unsqueeze(2).broadcast_to((R, 3, n))
            step(dve.tensor_copy(coarse[rows, :, 0:EG], logit[rows, :, 0:EG]))
            for t in range(3):
                step(dve.max(cmax[rows, t, :], coarse[rows, t, :]))
                step(dve.max_index(cidx[rows, t, :], cmax[rows, t, :], coarse[rows, t, :]))
            dve.tensor_tensor(ex4[rows], logit[rows, :, 0:EG], cmax[rows, :, 0:1].broadcast_to((R, 3, EG)), SUB
                              ).then_inc(s_rt, 1)
            p_group, group, w0, w1, e0, e1, i0, i1, tot = (col[i] for i in (0, 1, 4, 5, 6, 7, 8, 9, 10))
            diff = col[3]
            step(dve.tensor_copy(group[rows].unsqueeze(2), cidx[rows, :, 0:1]))
            tt(one4[rows], iota[rows, 0:EG].unsqueeze(1).broadcast_to((R, 3, EG)), three(group, EG), EQ)
            for t in range(3):
                tt(prod[rows, t], logit[rows, t, EG:].rearrange("p (g e) -> p e g", g=EG),
                   one4[rows, t].unsqueeze(1).broadcast_to((R, EL, EG)), MUL)
            step(dve.tensor_reduce(fine_sel[rows], prod[rows], AX.X, ADD))
            for t in range(3):
                step(dve.max(fmax[rows, t, :], fine_sel[rows, t, :]))
                step(dve.max_index(fidx[rows, t, :], fmax[rows, t, :], fine_sel[rows, t, :]))
            dve.tensor_tensor(diff[rows].unsqueeze(2), fmax[rows, :, 1:2], fmax[rows, :, 0:1], SUB).then_inc(s_rt, 1)
            step(dve.tensor_copy(i0[rows].unsqueeze(2), fidx[rows, :, 0:1]))
            step(dve.tensor_copy(i1[rows].unsqueeze(2), fidx[rows, :, 1:2]))
            stt(e0[rows], group[rows], float(EL), i0[rows], MUL, ADD)
            stt(e1[rows], group[rows], float(EL), i1[rows], MUL, ADD)
            many = lambda v: v[rows].unsqueeze(1).broadcast_to((R, E, 3))
            experts_i = iota[rows, 0:E].unsqueeze(2).broadcast_to((R, E, 3))
            tt(hot[1][rows], experts_i, many(e0), EQ)
            tt(hot[2][rows], experts_i, many(e1), EQ)
            dve.tensor_tensor(hot[0][rows], hot[1][rows], hot[2][rows], ADD).then_inc(s_mask, 1)
            dve.wait_ge(s_ex, 1)
            step(dve.tensor_reduce(tot[rows], ex4[rows], AX.X, ADD))
            step(dve.reciprocal(p_group[rows], tot[rows]))
            dve.wait_ge(s_ex, 2)
            ts(tot[rows], diff[rows], 1.0, ADD)
            step(dve.reciprocal(w0[rows], tot[rows]))
            tt(w0[rows], w0[rows], p_group[rows], MUL)
            tt(w1[rows], w0[rows], diff[rows], MUL)
            tt(hot[1][rows], hot[1][rows], many(w0), MUL)
            tt(hot[2][rows], hot[2][rows], many(w1), MUL)
            step(dve.memset(gates, 0.0))
            step(dve.memset(rank, -1.0))
            tt(gates[rows, 0:E, :], hot[1][rows], hot[2][rows], ADD)
            dve.wait_ge(s_mask, 1)
            dve.wait_ge(s_rank, 1)
            for t in range(3):
                rw = slice(0, TR[t])
                stt(rank[rw, 0:E, t], bank[7][rw, E * t:E * t + E], 1.0, hot[0][rw, :, t], ADD, MUL)
                ts(rank[rw, 0:E, t], rank[rw, 0:E, t], -1.0, ADD)
            step(dve.tensor_reduce(tot[0:1, 0:1], bank[7][0:1, E * 3:E * 4], AX.X, ALU.max))
            dve.tensor_copy(count_sb[0:1, 0:1], tot[0:1, 0:1]).then_inc(s_count, 1)
            for t in range(3):
                dve.tensor_scalar(xn[0:TR[t], t, :], xn[0:TR[t], t, :], rs[0:TR[t], t:t + 1], None, MUL
                                  ).then_inc(s_xn, 1)
            dve.wait_ge(s_count, 1)
            dve.wait_ge(s_res, KT)

            def picks(r, q):
                n = r * NPAIR + q
                need(dve, s_gath, n * 4)
                two_e = bass.ds(q * 2, 2)
                full = (R, 3, 2, SL)
                slots = iota[rows].unsqueeze(1).unsqueeze(1).broadcast_to(full)
                ranks = rank[rows, two_e, :].rearrange("p e t -> p t e").unsqueeze(3).broadcast_to(full)
                weights = gates[rows, two_e, :].rearrange("p e t -> p t e").unsqueeze(3).broadcast_to(full)
                dve.tensor_tensor(pick[rows], slots, ranks, EQ).then_inc(s_pk, 1)
                dve.wait_ge(s_pk, n + 1)
                dve.tensor_tensor(pick_g[rows], pick[rows], weights, MUL).then_inc(s_pick, 1)

            def gathered(n, par, xs):
                for x in xs:
                    if x == 0:
                        dve.wait_ge(s_pgt, n + 1)
                        dve.tensor_copy(pick_t[par], bank[3][:, 0:T]).then_inc(s_pgte, 1)
                    dve.wait_ge(s_gath, n * 4 + (x + 1))
                    dve.tensor_tensor(xg[:, 4 * x:4 * x + 4, :],
                                      bank[6 + x % 2][:, :].rearrange("p (k s) -> p k s", k=4),
                                      g_ffn[:, 4 * x:4 * x + 4].unsqueeze(2).broadcast_to((P, 4, 2 * SL)), MUL
                                      ).then_inc(s_xg, 1)

            def add_pair(n):
                for k in range(KT):
                    dve.wait_ge(s_sc, n * KT + (k + 1))
                    dve.tensor_tensor(hT[:, k, :], hT[:, k, :], bank[6 + k % 2][:, 0:T], ADD).then_inc(s_acc, 1)

            def hidden(e, j):
                dve.wait_ge(s_silu, e + 1)
                dve.tensor_tensor(hid[j], silu_s, bank[2][:, :].rearrange("p (f s) -> p f s", f=FT)[:, :, SL:], MUL
                                  ).then_inc(s_hid, 1)

            def expert_pass(r):
                picks(r, 0)
                gathered(r * NPAIR, 0, range(4))

                def experts(it):
                    for pr in range(2):
                        q = it * 2 + pr
                        n = r * NPAIR + q
                        more = not (isinstance(q, int) and q == NPAIR - 1)
                        if more:
                            picks(r, q + 1)
                        if not (isinstance(q, int) and q == 0):
                            add_pair(n - 1)
                        hidden(n * 2, 0)
                        if more:
                            gathered(n + 1, 1 - pr, (0, 1))
                        hidden(n * 2 + 1, 1)
                        if more:
                            gathered(n + 1, 1 - pr, (2, 3))

                runs(dve, E // 4, experts, 1)
                add_pair(r * NPAIR + (NPAIR - 1))

            def over(passes):
                dve.wait_ge(s_acc, passes * NPAIR * KT)
                dve.memset(pick_t[1], 0.0).then_inc(s_moe, 1)

            s_pk, s_less = sem("pick_step"), sem("ranks_lowered")
            expert_pass(0)
            most = dve.value_load(count_sb[0:1, 0:1], min_val=0, max_val=T)
            with dve.If(most > SL):
                with dve.Fori(1, NPASS) as r:
                    dve.tensor_scalar(rank, rank, -float(SL), None, ADD).then_inc(s_less, 1)
                    dve.wait_ge(s_less, r)
                    expert_pass(r)
                over(NPASS)
            with dve.Else():
                over(1)

            for n in range(12):
                t, k0 = n // 4, 4 * (n % 4)
                dve.wait_ge(s_fps, n + 1)
                dve.tensor_copy(xn[0:TR[t], t, P * k0:P * (k0 + 4)], bank[n % 4][0:TR[t], :]).then_inc(s_fev, 1)
            dve.wait_ge(s_fsq, 3)
            rms(3)
            dve.wait_ge(s_gf, 16)
            for t in range(3):
                dve.scalar_tensor_tensor(out=f_out[0:TR[t], t, :], in0=xn[0:TR[t], t, :], scalar=rs[0:TR[t], t:t + 1],
                                         in1=g_final[0:TR[t]], op0=MUL, op1=MUL).then_inc(s_o, 1)


_INS = ["x", "meta_tokens", "norm_mix", "norm_ffn", "norm_final", "s5_w_in", "s5_a_re", "s5_a_im", "s5_log_dt",
        "s5_b_re", "s5_b_im", "s5_c_re", "s5_c_im", "s5_d", "s5_w_glu", "moe_w_coarse", "moe_b_coarse",
        "moe_w_fine", "moe_b_fine", "moe_w_gate", "moe_w_up", "moe_w_down"]


def kernel(**inputs):
    import numpy as _np
    import concourse.bacc as _bacc
    from concourse import mybir as _mybir
    from concourse.bass_utils import run_bass_kernel_spmd as _run

    nc = _bacc.Bacc("TRN2", target_bir_lowering=False, num_devices=1)
    arrays, args = {}, {}
    for name in _INS:
        v = _np.ascontiguousarray(inputs[name])
        arrays[f"in_{name}"] = v
        args[name] = nc.dram_tensor(f"in_{name}", v.shape, _mybir.dt.from_np(v.dtype), kind="ExternalInput").ap()
    out = nc.dram_tensor("out_0", (1, SEQ, D), F32, kind="ExternalOutput").ap()
    trunk(nc, args, out)
    r = _run(nc, [arrays], core_ids=[0])
    return r.results[0]["out_0"]
```

```python
from contextlib import ExitStack
import math

import concourse.bass as bass
from concourse import mybir

F32 = mybir.dt.float32
I32 = mybir.dt.int32
U32 = mybir.dt.uint32
ALU = mybir.AluOpType
ACT = mybir.ActivationFunctionType
AX = mybir.AxisListType

P = 128
D = 2048
KT = D // P
META = 16
SEQ = 256
T = META + SEQ
L = 8
C = T // L
MC = META // L
G = 128
H = 16
NS = 64
GT = P // H
TR = [3 * C, 3 * C, 2 * C]
TO = [0, 3 * C, 6 * C]
R = TR[0]
E = 32
EG = 4
EL = 8
FE = 512
FT = FE // P
SL = 64
NPASS = -(-T // SL)
NPAIR = E // 2
UNIT = 4096
EPS = 1e-6
ROUND = 12582912.0
TWO_PI = 6.2831845
INV_2PI = 1.0 / (2.0 * math.pi)
EXP_FLOOR = -32.0


def trunk(nc, a, out):
    ctx = ExitStack()
    with ctx:
        arena = ctx.enter_context(nc.sbuf_tensor("arena", [P, 53200], F32))
        count_sb = ctx.enter_context(nc.sbuf_tensor("count_sb", [1, 1], I32))
        bank = [ctx.enter_context(nc.psum_tensor(f"bank{i}", [P, 512], F32)) for i in range(8)]

        def sem(name):
            return ctx.enter_context(nc.semaphore(name))

        def at(base, *dims):
            n = 1
            for d in dims:
                n *= d
            v = arena[:, base:base + n]
            if len(dims) == 1:
                return v
            names = "abcd"[:len(dims)]
            return v.rearrange(f"p ({' '.join(names)}) -> p {' '.join(names)}",
                               **{names[i]: dims[i] for i in range(1, len(dims))})

        def carver(base, end):
            pos = [base]

            def carve(*dims):
                v = at(pos[0], *dims)
                for_size = 1
                for d in dims:
                    for_size *= d
                pos[0] += for_size
                assert pos[0] <= end, (pos[0], end)
                return v
            return carve

        RING, RES = 0, 8 * UNIT
        REG2 = RES + KT * T
        REG3 = REG2 + 3 * D
        CONST = 53200 - 512
        slot = [at(RING + i * UNIT, UNIT) for i in range(8)]
        hT = at(RES, KT, T)

        const = carver(CONST, 53200)
        ident = const(P)
        iota = const(SL)
        notfirst = const(C)
        turn = const(P)
        g_mix = const(KT)
        g_ffn = const(KT)
        d_skip = const(KT)
        stat = const(12)
        preload = const(1)
        round_c, quarter = const(1), const(1)
        stat3 = [stat[0:R, 3 * i:3 * i + 3] for i in range(4)]
        rs_final = stat3[3]

        s5a = carver(RING + 4 * UNIT, RING + 8 * UNIT)
        b1, b2, c1, c2 = s5a(H, G), s5a(H, G), s5a(H, G), s5a(H, G)
        hsT = s5a(KT, T)
        pow_re, pow_im = s5a(L + 1, G), s5a(L + 1, G)
        rho8, phi8 = s5a(G), s5a(G)
        u_sb = [s5a(T) for _ in range(2)]
        u_ch = [s5a(GT, C) for _ in range(2)]

        s5b = carver(RING + 2 * UNIT, RING + 4 * UNIT)
        w_tmp, g_tmp = s5b(GT, L + 1, H), s5b(GT, L, H)
        cos_t = [s5b(GT, C) for _ in range(2)]
        sin_t = [s5b(GT, C) for _ in range(2)]
        mag_t = [s5b(GT, C) for _ in range(2)]
        frac, whole = s5b(GT, C), s5b(GT, C)
        s_sb, t1, t2, zz = s5b(GT, C), s5b(GT, C), s5b(GT, C), s5b(GT, C)
        x_prev = s5b(GT, C + 1)
        y_sb = s5b(GT, C)
        y_ch = [s5b(T) for _ in range(2)]
        diag, ones_a = s5b(3, R), s5b(P)
        small = [s5b(NS) for _ in range(16)]

        nat = carver(REG3, CONST)
        b_raw = nat(2, NS, H)
        b_nat = nat(3, NS, H)
        c_nat = nat(H, 3, NS)
        nat4 = nat(4, 2, NS)
        p_tmp = nat(4, G)

        s5c = carver(REG3, CONST)
        w_sb = [s5c(GT, L + 1, H) for _ in range(2)]
        g_sb, gt_sb = s5c(GT, L, H), s5c(GT, P)
        t_sb = s5c(GT, L, H)
        b_rep = s5c(GT, L + 1, H)
        u_ch += [s5c(GT, C) for _ in range(2)]

        h_nat = at(REG2, 3, D)
        zT = at(REG2, KT, T)
        glu = carver(REG2 + KT * T, REG3)
        w_router = glu(KT, EG + E)
        b_router = glu(EG + E)
        sumsq = glu(3, KT)

        moe = carver(REG3, CONST)
        xn = moe(3, D)
        h_new = [moe(T) for _ in range(2)]
        gate_s = [moe(T) for _ in range(2)]
        value_s = moe(T)
        rank = moe(E, 3)
        gates = moe(E, 3)
        square_s = moe(P)
        fin_sq = moe(3, 4)
        moe2 = carver(REG3 + 3 * D, REG3 + 3 * D + 5 * T)
        pick, pick_g = moe2(3, 2, SL), moe2(3, 2, SL)
        pick_t = [moe(T) for _ in range(2)]

        rt = carver(REG2, REG2 + KT * T)
        logit = rt(3, EG + E)
        coarse, fine_sel = rt(3, EL), rt(3, EL)
        prod = rt(3, EL, EG)
        cmax, fmax = rt(3, 8), rt(3, 8)
        cidx, fidx = rt(3, 8).bitcast(U32), rt(3, 8).bitcast(U32)
        one4, ex4 = rt(3, EG), rt(3, EG)
        col = [rt(3) for _ in range(12)]
        hot = [rt(E, 3) for _ in range(3)]
        before, ones = rt(R), rt(R)

        m2 = carver(REG2, REG3)
        xg = m2(KT, 2 * SL)
        y_pair = m2(D)
        hid = [m2(FT, SL) for _ in range(2)]
        silu_s = m2(FT, SL)
        gu_s = [m2(FE) for _ in range(2)]

        s_h = [sem(f"h_loaded{t}") for t in range(3)]
        s_par, s_vec, s_gains, s_router = (sem("b_loaded"), sem("vectors_loaded"), sem("gains_loaded"),
                                           sem("router_loaded"))
        s_cneg, s_rsrow = sem("c_negated"), sem("rs_row_done")
        s_cpar, s_uout, s_yout = sem("c_loaded"), sem("u_in_dram"), sem("y_in_dram")
        ring = [sem(f"ring_full{i}") for i in range(8)]
        s_const, s_rep0, s_t0, s_x0, s_stat = (sem("constants_ready"), sem("b_rep_cleared"), sem("t_cleared"),
                                               sem("x_prev_cleared"), sem("stat_set"))
        s_pool, s_dve, s_root = sem("pool_step"), sem("vector_step"), sem("root_ready")
        s_sq, s_rs, s_diag = sem("squares_summed"), sem("mean_inverse_ready"), sem("diag_ready")
        s_hps, s_hev, s_gev = sem("h_transposed"), sem("h_copied"), sem("hs_copied")
        s_ang, s_trig, s_n4, s_n4t, s_rho, s_pow = (sem("angle_ready"), sem("trig_ready"), sem("nat4_ready"),
                                                    sem("nat4_transposed"), sem("nat4_copied"), sem("powers_ready"))
        s_bc, s_bct, s_bce = sem("b_stacks_ready"), sem("stacks_transposed"), sem("stacks_copied")
        s_u, s_uev, s_uch, s_du = sem("u_done"), sem("u_copied"), sem("u_shuffled"), sem("du_ready")
        s_wt, s_w, s_gp, s_g, s_gt, s_gte, s_rep = (sem("w_step"), sem("w_ready"), sem("g_step"), sem("g_ready"),
                                                    sem("g_transposed"), sem("g_copied"), sem("b_rep_ready"))
        s_tp, s_fr, s_sn, s_tab = (sem("table_step"), sem("phase_ready"), sem("sine_step"),
                                         sem("tables_ready"))
        s_s, s_sev, s_qs, s_ch, s_zz, s_qz, s_xp = (sem("s_done"), sem("s_copied"), sem("s_turned"), sem("chain_step"),
                                                    sem("scan_done"), sem("z_turned"), sem("x_prev_ready"))
        s_t, s_tev, s_y, s_yev, s_ych, s_z = (sem("t_done"), sem("t_copied"), sem("y_done"), sem("y_copied"),
                                              sem("y_shuffled"), sem("y_ready"))
        s_gelu, s_glu, s_sig, s_gl, s_new, s_res = (sem("gelu_done"), sem("glu_done"), sem("gate_ready"),
                                                    sem("gated_ready"), sem("h_new_ready"), sem("residual_written"))
        s_nps, s_nev, s_log, s_gw, s_ssz, s_ssp = (sem("h_new_transposed"), sem("h_new_natural"), sem("logits_added"),
                                                   sem("router_scaled"), sem("partial_cleared"), sem("partial_squares"))
        s_tri, s_mask, s_rank, s_count, s_rt, s_ex = (
            sem("triangle_ready"), sem("mask_ready"), sem("rank_done"), sem("count_ready"),
            sem("exponents_ready"), sem("exponentials_ready"))
        s_pick, s_pgt, s_pgte, s_gath, s_xg = (sem("pick_ready"), sem("pick_transposed"),
                                                       sem("pick_copied"), sem("gathered"), sem("xg_copied"))
        s_gu, s_guc, s_gut, s_silu, s_hid = (sem("gate_up_done"), sem("gate_up_copied"), sem("gate_up_transposed"),
                                             sem("silu_done"), sem("hidden_ready"))
        s_yp, s_ye, s_sc, s_acc = sem("down_done"), sem("down_copied"), sem("scattered"), sem("added")
        s_fin, s_fadd, s_scaled, s_rsf, s_oa = (sem("final_scattered"), sem("final_added"), sem("final_gained"),
                                                sem("rs_ready"), sem("out_ready_scalar"))
        s_moe, s_fps, s_fev, s_fsq, s_gf, s_o, s_out = (sem("moe_over"), sem("final_transposed"), sem("final_copied"),
                                                        sem("final_squares"), sem("g_final_loaded"),
                                                        sem("out_ready"), sem("out_stored"))

        def need(eng, s, n):
            if not (isinstance(n, int) and n <= 0):
                eng.wait_ge(s, n)

        def runs(eng, n, body, last):
            body(0)
            with eng.Fori(1, n - last) as it:
                body(it)
            if last:
                body(n - 1)

        u_dram = [nc.dram_tensor(f"u_dram{i}", (P, T), F32).ap() for i in range(2)]
        y_dram = [nc.dram_tensor(f"y_dram{i}", (P, T), F32).ap() for i in range(2)]
        x_steps = a["x"].rearrange("b (c s) d -> (b s) c d", s=L)
        meta_steps = a["meta_tokens"].rearrange("(c s) d -> s c d", s=L)
        w_in = a["s5_w_in"].rearrange("a (k p) (n w) -> p (a n) k w", p=P, w=256)
        w_glu = a["s5_w_glu"].rearrange("a (k p) (n w) -> p (a n) k w", p=P, w=256)
        w_gu = [a[n].rearrange("a e (i k p) f -> p (a e i) k f", p=P, i=2) for n in ("moe_w_gate", "moe_w_up")]
        w_dn = a["moe_w_down"].rearrange("a e (i f p) d -> p (a e i) f d", p=P, i=2)
        out_steps = out.rearrange("b (c s) d -> (b s) c d", s=L)

        def in_slot(i):
            return slot[i].rearrange("p (k w) -> p k w", k=KT)

        def gu_slot(i):
            return slot[i].rearrange("p (k f) -> p k f", k=KT // 2)

        def dn_slot(i):
            return slot[i].rearrange("p (f d) -> p f d", f=2)

        def one(v, m):
            v = v[:, bass.ds(m, 1)]
            names = " ".join("abcd"[:v.ndim - 2])
            return v.rearrange(f"p x {names} -> p (x {names[0]}) {names[1:]}".rstrip())

        def flat(v):
            return v.rearrange("p g c -> p (g c)")

        g_final = slot[0][0:R, 0:D]
        f_out = at(RING + UNIT, 3, D)
        f_junk = at(RING + 3 * UNIT, 8, D // 4)
        F_BANK = (6, 7, 0, 1)
        D_BANK = (2, 3, 4, 5)

        BEFORE = [8, 8, 4, 4, 0, 0, 0, 0]

        block = ctx.enter_context(nc.Block())

        @block.sync
        def _(sp):
            for s in range(L):
                t, r0 = s // 3, (s % 3) * C
                sp.dma_start(h_nat[r0:r0 + MC, t, :], meta_steps[s]).then_inc(s_h[t], 16)
                sp.dma_start(h_nat[r0 + MC:r0 + C, t, :], x_steps[s]).then_inc(s_h[t], 16)
            for n in range(2):
                sp.dma_start(in_slot(n), w_in[:, n]).then_inc(ring[n], 16)

            def u_send(m, j):
                sp.wait_ge(s_uev, m + 1)
                sp.dma_start(u_dram[j % 2], u_sb[j % 2]).then_inc(s_uout, 16)

            def u_fetch(m, j):
                sp.wait_ge(s_uout, (m + 1) * 16)
                for s in range(L):
                    q = L - 1 - s
                    sp.dma_start(u_ch[j % 4][H * q:H * q + H],
                                 u_dram[j % 2].rearrange("(g h) (s c) -> s h g c", g=GT, s=L)[s]
                                 ).then_inc(s_uch, 16)

            def y_send(m, j):
                sp.wait_ge(s_yev, m + 1)
                sp.dma_start(y_dram[j % 2], flat(y_sb)).then_inc(s_yout, 16)

            def y_fetch(m, j):
                sp.wait_ge(s_yout, (m + 1) * 16)
                for g in range(GT):
                    sp.dma_start(y_ch[j % 2][H * g:H * g + H].rearrange("h (t c) -> h t c", t=L),
                                 y_dram[j % 2].rearrange("(t h) (g c) -> g h t c", t=L, g=GT)[g]
                                 ).then_inc(s_ych, 16)

            u_send(0, 0)
            u_fetch(0, 0)
            u_send(1, 1)
            u_fetch(1, 1)

            def tiles(it):
                last = isinstance(it, int) and it == 3
                for j in range(4):
                    m = it * 4 + j
                    if j % 2 == 0 and not last:
                        unit = sp.snap(it * 2 + (j // 2 + 2))
                        sp.wait_ge(s_u, m + 2)
                        sp.dma_start(in_slot(j // 2), one(w_in, unit)).then_inc(ring[j // 2], 16)
                    if not (last and j >= 2):
                        u_send(m + 2, j + 2)
                        u_fetch(m + 2, j + 2)
                    y_send(m, j)
                    if last and j == 1:
                        sp.wait_ge(s_u, KT)
                        for i in range(2):
                            sp.dma_start(in_slot(i), w_glu[:, 8 * i]).then_inc(ring[i], 16)
                    y_fetch(m, j)

            runs(sp, 4, tiles, 1)
            sp.wait_ge(s_z, KT)
            for i in range(2):
                sp.dma_start(in_slot(2 + i), w_glu[:, 1 + 8 * i]).then_inc(ring[2 + i], 16)
            sp.dma_start(w_router[:, :, 0:EG], a["moe_w_coarse"].rearrange("a (k p) e -> p (a k) e", p=P)
                         ).then_inc(s_router, 16)
            sp.dma_start(w_router[:, :, EG:], a["moe_w_fine"].rearrange("a (k p) e -> p (a k) e", p=P)
                         ).then_inc(s_router, 16)
            sp.dma_start(b_router[:, 0:EG], a["moe_b_coarse"].to_broadcast((P, EG))).then_inc(s_router, 16)
            sp.dma_start(b_router[:, EG:], a["moe_b_fine"].to_broadcast((P, E))).then_inc(s_router, 16)

            def expert_stage(q, g, s2):
                if g < 4:
                    unit = sp.snap(q * 4 + g) if not isinstance(q, int) else q * 4 + g
                    sp.dma_start(gu_slot(s2), one(w_gu[0], unit)).then_inc(ring[s2], 16)
                    sp.dma_start(gu_slot(s2 + 1), one(w_gu[1], unit)).then_inc(ring[s2 + 1], 16)
                else:
                    for x in range(2):
                        sp.dma_start(dn_slot(s2 + x), one(w_dn, q * 4 + (2 * x + g - 4))).then_inc(ring[s2 + x], 16)

            def glu_pairs(it):
                for b in range(2):
                    unit = sp.snap(it * 2 + (b + 2))
                    sp.wait_ge(s_glu, it * 4 + (2 * b + 2))
                    sp.dma_start(in_slot(2 * b), one(w_glu, unit)).then_inc(ring[2 * b], 16)
                    sp.dma_start(in_slot(2 * b + 1), one(w_glu, unit + 8)).then_inc(ring[2 * b + 1], 16)

            glu_pairs(0)
            expert_stage(0, 2, 4)
            expert_stage(0, 3, 6)
            with sp.Fori(1, 3) as it:
                glu_pairs(it)
            sp.wait_ge(s_glu, 14)
            expert_stage(0, 0, 0)
            sp.wait_ge(s_glu, 16)
            expert_stage(0, 1, 2)

            def slots_used(q, g):
                if g < 4:
                    sp.wait_ge(s_gu, q * 4 + (g + 1))
                else:
                    sp.wait_ge(s_yp, q * 4 + 4)

            def expert_pass(r):
                if not isinstance(r, int):
                    for n in range(4):
                        slots_used(r * NPAIR - 1, n + 2)
                        expert_stage(0, n, 2 * n)
                with sp.Fori(0, NPAIR // 2 - 1) as it:
                    for n in range(12):
                        slots_used(r * NPAIR + it * 2 + n // 6, n % 6)
                        expert_stage(it * 2 + (n + 4) // 6, (n + 4) % 6, 2 * (n % 4))
                for n in range(6 * NPAIR - 8, 6 * NPAIR):
                    slots_used(r * NPAIR + (n - 4) // 6, (n - 4) % 6)
                    expert_stage(n // 6, n % 6, 2 * (n % 4))

            def load_g_final():
                sp.dma_start(g_final, a["norm_final"].rearrange("(a d) -> a d", a=1).to_broadcast((R, D))
                             ).then_inc(s_gf, 16)

            def store(also):
                for s in range(L):
                    t, r0 = s // 3, (s % 3) * C
                    sp.wait_ge(s_o, t + 1)
                    if also:
                        sp.wait_ge(s_oa, t + 1)
                    sp.dma_start(out_steps[s], f_out[r0 + MC:r0 + C, t, :]).then_inc(s_out, 16)
                sp.wait_ge(s_out, 16 * L)

            expert_pass(0)
            sp.wait_ge(s_count, 1)
            most = sp.value_load(count_sb[0:1, 0:1], min_val=0, max_val=T)
            with sp.If(most > SL):
                with sp.Fori(1, NPASS) as r:
                    expert_pass(r)
                sp.wait_ge(s_yp, NPASS * (NPAIR * 4))
                load_g_final()
                store(False)
            with sp.Else():
                sp.wait_ge(s_gu, NPAIR * 4)
                load_g_final()
                store(True)

        @block.gpsimd
        def _(pool):
            steps = [0]

            def step(ins):
                steps[0] += 1
                ins.then_inc(s_pool, 1)
                pool.wait_ge(s_pool, steps[0])

            step(pool.memset(ident, 0.0))
            step(pool.affine_select(out=ident, in_=ident, compare_op=ALU.not_equal, fill=1.0, base=0,
                                    pattern=[[-1, P]], channel_multiplier=1))
            step(pool.memset(turn, 0.0))
            step(pool.affine_select(out=turn, in_=turn, compare_op=ALU.not_equal, fill=1.0, base=-NS,
                                    pattern=[[-1, P]], channel_multiplier=1))
            step(pool.affine_select(out=turn, in_=turn, compare_op=ALU.not_equal, fill=-1.0, base=NS,
                                    pattern=[[-1, P]], channel_multiplier=1))
            step(pool.iota(iota, pattern=[[1, SL]], base=0, channel_multiplier=0,
                           allow_small_or_imprecise_dtypes=True))
            step(pool.tensor_scalar(notfirst, iota[:, 0:C], 1.0, None, ALU.min))
            pool.memset(x_prev, 0.0).then_inc(s_x0, 1)
            pool.memset(stat, 1.0).then_inc(s_stat, 1)
            step(pool.memset(round_c, ROUND))
            step(pool.memset(quarter, math.pi / 2))
            step(pool.memset(ones_a, 1.0))
            pool.iota(iota, pattern=[[1, SL]], base=0, channel_multiplier=0,
                      allow_small_or_imprecise_dtypes=True).then_inc(s_const, 1)
            pool.dma_start(c_nat[:, :, 0, :], a["s5_c_re"].rearrange("a g h n -> (a g) h n")).then_inc(s_cpar, 16)
            pool.dma_start(c_nat[:, :, 1, :], a["s5_c_im"].rearrange("a g h n -> (a g) h n")).then_inc(s_cpar, 16)
            pool.wait_ge(s_cpar, 16 * 2)
            pool.tensor_scalar(c_nat[:, :, 2, :], c_nat[:, :, 0, :], -1.0, None, ALU.mult).then_inc(s_cneg, 1)
            pool.tensor_scalar(c_nat[:, :, 1, :], c_nat[:, :, 1, :], -1.0, None, ALU.mult).then_inc(s_cneg, 1)

            def tables(m, j):
                ph = phi8[:, bass.ds(m * GT, GT)].unsqueeze(2).broadcast_to((P, GT, C))
                rh = rho8[:, bass.ds(m * GT, GT)].unsqueeze(2).broadcast_to((P, GT, C))
                io = iota[:, 0:C].unsqueeze(1).broadcast_to((P, GT, C))
                nf = notfirst.unsqueeze(1).broadcast_to((P, GT, C))
                rc = round_c.unsqueeze(2).broadcast_to((P, GT, C))
                need(pool, s_tab, m)
                need(pool, s_xp, m - 1)
                pool.tensor_tensor(frac, ph, io, ALU.mult).then_inc(s_tp, 1)
                pool.wait_ge(s_tp, m * 4 + 1)
                pool.tensor_tensor(whole, frac, rc, ALU.add).then_inc(s_tp, 1)
                pool.wait_ge(s_tp, m * 4 + 2)
                pool.tensor_tensor(whole, whole, rc, ALU.subtract).then_inc(s_tp, 1)
                pool.wait_ge(s_tp, m * 4 + 3)
                pool.tensor_tensor(frac, frac, whole, ALU.subtract).then_inc(s_fr, 1)
                pool.tensor_tensor(mag_t[j % 2], rh, nf, ALU.mult).then_inc(s_tp, 1)

            def g_of(m):
                full = (P, GT, L, H)
                g0 = bass.ds(m * GT, GT)
                pr = pow_re[:, 0:L, g0].rearrange("p q g -> p g q").unsqueeze(3).broadcast_to(full)
                pi = pow_im[:, 0:L, g0].rearrange("p q g -> p g q").unsqueeze(3).broadcast_to(full)
                v1 = b1[:, :, g0].rearrange("p h g -> p g h").unsqueeze(2).broadcast_to(full)
                v2 = b2[:, :, g0].rearrange("p h g -> p g h").unsqueeze(2).broadcast_to(full)
                need(pool, s_g, m)
                pool.tensor_tensor(g_tmp, v2, pi, ALU.mult).then_inc(s_gp, 1)
                need(pool, s_gt, m)
                pool.tensor_tensor(g_sb, v1, pr, ALU.mult).then_inc(s_gp, 1)
                pool.wait_ge(s_gp, m * 2 + 2)
                pool.tensor_tensor(g_sb, g_sb, g_tmp, ALU.add).then_inc(s_g, 1)

            def rep_of(m):
                pool.wait_ge(s_rep0, 1)
                need(pool, s_t, m)
                v = b1[:, :, bass.ds(m * GT, GT)].rearrange("p h g -> p g h").unsqueeze(2)
                pool.tensor_copy(b_rep[:, :, 0:L + 1:2, :], v.broadcast_to((P, GT, L // 2 + 1, H))).then_inc(s_rep, 1)

            pool.wait_ge(s_rho, 4)
            tables(0, 0)
            pool.wait_ge(s_bce, 8)
            pool.wait_ge(s_pow, 1)
            g_of(0)
            pool.wait_ge(s_bce, 16)
            pool.memset(b_rep, 0.0).then_inc(s_rep0, 1)
            rep_of(0)
            pool.memset(t_sb, 0.0).then_inc(s_t0, 1)

            g_of(1)

            def tiles(it):
                for j in range(4):
                    m = it * 4 + j
                    if isinstance(m, int) and m == 0:
                        continue
                    tables(m, j)
                    if not (isinstance(m, int) and m == KT - 1):
                        g_of(m + 1)
                    rep_of(m)

            runs(pool, 4, tiles, 1)

            def residuals(it):
                for j in range(4):
                    m = it * 4 + j
                    pool.wait_ge(s_const, 1)
                    pool.wait_ge(s_new, m + 1)
                    pool.tensor_copy(one_res(m), h_new[j % 2]).then_inc(s_res, 1)

            def one_res(m):
                return hT[:, bass.ds(m, 1), :].rearrange("p a t -> p (a t)")

            runs(pool, 4, residuals, 0)
            pool.wait_ge(s_glu, KT)
            step(pool.memset(ones, 1.0))
            pool.affine_select(out=before, in_=ones, compare_op=ALU.is_gt, fill=0.0, base=0,
                               pattern=[[1, R]], channel_multiplier=-1).then_inc(s_tri, 1)

        @block.scalar
        def _(act):
            act.dma_start(small[0], a["s5_a_re"].rearrange("a g n -> (a g) n")).then_inc(s_vec, 16)
            act.dma_start(small[1], a["s5_a_im"].rearrange("a g n -> (a g) n")).then_inc(s_vec, 16)
            with nc.allow_non_contiguous_dma(reason="small vectors, one element per partition and tile"):
                act.dma_start(small[2][:, 0:1], a["s5_log_dt"].rearrange("a g -> g a")).then_inc(s_vec, 16)
            act.dma_start(b_raw[:, 0], a["s5_b_re"].rearrange("a g n h -> (a g) n h")).then_inc(s_par, 16)
            act.dma_start(b_raw[:, 1], a["s5_b_im"].rearrange("a g n h -> (a g) n h")).then_inc(s_par, 16)
            with nc.allow_non_contiguous_dma(reason="small vectors, one element per partition and tile"):
                act.dma_start(g_mix, a["norm_mix"].rearrange("a (k p) -> p (a k)", p=P)).then_inc(s_gains, 16)
                act.dma_start(d_skip, a["s5_d"].rearrange("a (k p) -> p (a k)", p=P)).then_inc(s_gains, 16)
                act.dma_start(g_ffn, a["norm_ffn"].rearrange("a (k p) -> p (a k)", p=P)).then_inc(s_gains, 16)

            act.wait_ge(s_ang, 1)
            act.activation(small[5], small[4], ACT.Sin, scale=TWO_PI).then_inc(s_trig, 1)
            act.activation(small[6], small[4], ACT.Sin, scale=TWO_PI / 2).then_inc(s_trig, 1)
            act.wait_ge(s_stat, 1)
            for t in range(3):
                act.wait_ge(s_h[t], 16 * 2 * (TR[t] // C))
                junk = hsT.rearrange("p k t -> p (k t)")[0:TR[t], 0:D]
                act.activation(junk, h_nat[0:TR[t], t, :], ACT.Square,
                               accum_out=stat3[0][0:TR[t], t:t + 1]).then_inc(s_sq, 1)
                act.wait_ge(s_sq, t + 1)
            for k in range(KT):
                if k == KT // 2:
                    act.wait_ge(s_rs, 1)
                    act.activation(stat3[2], stat3[1], ACT.Sqrt).then_inc(s_root, 1)
                act.wait_ge(s_hps, k + 1)
                act.activation(hT[:, k, :], bank[k % 4][:, 0:T], ACT.Copy).then_inc(s_hev, 1)

            def u_copy(m, j):
                act.wait_ge(s_u, m + 1)
                need(act, s_uout, (m - 1) * 16)
                need(act, s_du, m - 1)
                act.activation(u_sb[j % 2], bank[j % 2][:, 0:T], ACT.Copy).then_inc(s_uev, 1)

            def gt_copy(m):
                act.wait_ge(s_gt, m + 1)
                need(act, s_s, m)
                for i in range(2):
                    act.activation(gt_sb[:, 4 * i:4 * i + 4, :], bank[4 + i][:, :].rearrange("p (g n) -> p g n", g=4),
                                   ACT.Copy).then_inc(s_gte, 1)

            def t_copy(m):
                act.wait_ge(s_t, m + 1)
                if isinstance(m, int) and m == 0:
                    act.wait_ge(s_t0, 1)
                for b in (1, 0):
                    for i in range(4):
                        n = 2 + 2 * i
                        act.activation(t_sb[32 * i:32 * i + 32, 4 * b:4 * b + 4, L - n:L, :],
                                       bank[2 + b][32 * i:32 * i + 32, :].rearrange(
                                           "p (g v h) -> p g v h", g=4, v=L)[:, :, 0:n, :],
                                       ACT.Copy).then_inc(s_tev, 1)

            def s_copy(m):
                act.wait_ge(s_s, m + 1)
                need(act, s_ch, m * 5 - 4)
                act.activation(flat(s_sb), bank[3][:, 0:GT * C], ACT.Copy).then_inc(s_sev, 1)

            def sines(m, j):
                act.wait_ge(s_fr, m + 1)
                need(act, s_xp, m - 1)
                act.activation(sin_t[j % 2], frac, ACT.Sin, scale=TWO_PI).then_inc(s_sn, 1)
                act.activation(cos_t[j % 2], frac, ACT.Abs).then_inc(s_sn, 1)
                act.wait_ge(s_sn, m * 2 + 2)
                act.activation(cos_t[j % 2], cos_t[j % 2], ACT.Sin, bias=quarter, scale=-TWO_PI).then_inc(s_tab, 1)

            for i in range(16):
                act.wait_ge(s_bct, i + 1)
                dst = (b1, b2, c1, c2)[i // 4][:, 4 * (i % 4):4 * (i % 4) + 4, :]
                act.activation(dst, bank[2 + i % 4][:, :].rearrange("p (h g) -> p h g", h=4), ACT.Copy
                               ).then_inc(s_bce, 1)
            u_copy(0, 0)
            sines(0, 0)
            u_copy(1, 1)
            gt_copy(0)
            s_copy(0)
            t_copy(0)
            gt_copy(1)

            def gelu(i):
                act.wait_ge(s_z, 4 * i + 4)
                act.activation(zT[:, 4 * i:4 * i + 4, :], zT[:, 4 * i:4 * i + 4, :], ACT.Gelu_apprx_tanh
                               ).then_inc(s_gelu, 1)

            def tiles(it):
                last = isinstance(it, int) and it == 3
                for j in range(4):
                    m = it * 4 + j
                    if not (last and j == 3):
                        sines(m + 1, j + 1)
                    if not (last and j >= 2):
                        u_copy(m + 2, j)
                    if not (last and j == 3):
                        s_copy(m + 1)
                    if last and j == 3:
                        gelu(0)
                        gelu(1)
                    act.wait_ge(s_y, m + 1)
                    need(act, s_yout, m * 16)
                    act.activation(flat(y_sb), bank[7][:, 0:GT * C], ACT.Copy).then_inc(s_yev, 1)
                    if not (last and j == 3):
                        t_copy(m + 1)
                    if not (last and j >= 2):
                        gt_copy(m + 2)

            runs(act, 4, tiles, 1)

            gelu(2)
            gelu(3)

            def squares(m):
                act.wait_ge(s_nev, m * 2 + 2)
                for t in range(3):
                    need(act, s_ssp, m * 3 + t)
                    act.activation(square_s[0:TR[t], :], xn[0:TR[t], t, bass.ds(m * P, P)], ACT.Square,
                                   accum_out=sumsq[0:TR[t], t, bass.ds(m, 1)]).then_inc(s_ssp, 1)

            def glu_tiles(it):
                for j in range(4):
                    m = it * 4 + j
                    act.wait_ge(s_glu, m + 1)
                    need(act, s_gl, m - 1)
                    act.activation(gate_s[j % 2], bank[2 * (j % 2) + 1][:, 0:T], ACT.Sigmoid).then_inc(s_sig, 1)
                    if isinstance(m, int) and m == 0:
                        act.wait_ge(s_ssz, 1)
                    else:
                        squares(m - 1)

            runs(act, 4, glu_tiles, 0)
            squares(KT - 1)

            act.wait_ge(s_rs, 2)
            act.activation(stat3[2], stat3[1], ACT.Sqrt).then_inc(s_root, 1)
            act.wait_ge(s_rt, 1)
            act.activation(ex4[0:R], ex4[0:R], ACT.Exp).then_inc(s_ex, 1)
            act.wait_ge(s_rt, 2)
            act.activation(col[3][0:R], col[3][0:R], ACT.Exp).then_inc(s_ex, 1)

            def expert_pass(r, whole=True):
                def experts(it, final=False):
                    for j in range(4):
                        e = r * E + (it * 4 + j)
                        q = r * NPAIR + (it * 2 + j // 2)
                        act.wait_ge(s_gu, e * 2 + 2)
                        act.activation(gu_s[j % 2], bank[j % 2][:, :], ACT.Copy).then_inc(s_guc, 1)
                        act.wait_ge(s_gut, e + 1)
                        need(act, s_hid, e)
                        act.activation(silu_s, bank[2][:, :].rearrange("p (f s) -> p f s", f=FT)[:, :, 0:SL],
                                       ACT.Silu).then_inc(s_silu, 1)
                        if j % 2 == 1 and not (final and j == 3):
                            for c in range(4):
                                act.wait_ge(s_yp, q * 4 + (c + 1))
                                act.activation(y_pair[:, 512 * c:512 * c + 512], bank[4 + c % 2][:, :],
                                               ACT.Copy).then_inc(s_ye, 1)

                runs(act, E // 4 - (not whole), experts, 0)
                return experts

            def root_of_final():
                act.wait_ge(s_rs, 3)
                act.activation(stat3[2], stat3[1], ACT.Sqrt).then_inc(s_root, 1)

            experts_0 = expert_pass(0, whole=False)
            act.wait_ge(s_count, 1)
            most = act.value_load(count_sb[0:1, 0:1], min_val=0, max_val=T)
            with act.If(most > SL):
                experts_0(E // 4 - 1)
                with act.Fori(1, NPASS) as r:
                    expert_pass(r)
                for t in range(3):
                    act.wait_ge(s_fev, 4 * t + 4)
                    act.activation(f_out[0:TR[t], t, :], xn[0:TR[t], t, :], ACT.Square,
                                   accum_out=stat3[0][0:TR[t], t:t + 1]).then_inc(s_fsq, 1)
                root_of_final()
            with act.Else():
                experts_0(E // 4 - 1, final=True)
                for n in range(12):
                    c, t = n // 3, n % 3
                    act.wait_ge(s_fps, n + 1)
                    act.activation(xn[0:TR[t], t, 512 * c:512 * c + 512], bank[F_BANK[n % 4]][0:TR[t], :], ACT.Copy
                                   ).then_inc(s_fev, 1)
                act.activation(preload, quarter, ACT.Sqrt)
                for c in range(4):
                    act.wait_ge(s_yp, (NPAIR - 1) * 4 + (c + 1))
                    act.activation(y_pair[:, 512 * c:512 * c + 512], bank[D_BANK[c]][:, :], ACT.Copy).then_inc(s_ye, 1)
                for n in range(12):
                    c, t = n // 3, n % 3
                    act.wait_ge(s_fadd, n + 1)
                    need(act, s_fsq, n - 7)
                    act.activation(f_junk[0:TR[t], n % 8, :], xn[0:TR[t], t, 512 * c:512 * c + 512], ACT.Square,
                                   accum_out=fin_sq[0:TR[t], t, c:c + 1]).then_inc(s_fsq, 1)
                root_of_final()
                act.wait_ge(s_scaled, 6)
                act.wait_ge(s_rsf, 3)
                for t in range(3):
                    act.activation(f_out[0:TR[t], t, 0:D // 2], f_out[0:TR[t], t, 0:D // 2], ACT.Copy,
                                   scale=rs_final[0:TR[t], t:t + 1]).then_inc(s_oa, 1)

        @block.tensor
        def _(pe):
            pe.wait_ge(s_const, 1)
            for t in range(3):
                pe.wait_ge(s_h[t], 16 * 2 * (TR[t] // C))
            for k in range(KT):
                need(pe, s_hev, k - 3)
                for t in range(3):
                    last = pe.transpose(bank[k % 4][:, TO[t]:TO[t] + TR[t]], h_nat[0:TR[t], t, P * k:P * k + P],
                                        ident[0:TR[t], 0:TR[t]])
                last.then_inc(s_hps, 1)

            def u_product(m, j, s2, n, between=lambda k: None):
                pe.wait_ge(ring[s2], n * 16)
                need(pe, s_uev, m - 1)
                for k in range(KT):
                    last = pe.matmul(bank[j % 2][:, 0:T], in_slot(s2)[:, k, P * (j % 2):P * (j % 2) + P],
                                     hsT[:, k, :], start=(k == 0), stop=(k == KT - 1))
                    if k == KT - 1:
                        last.then_inc(s_u, 1)
                    between(k)

            def g_transpose(m):
                pe.wait_ge(s_g, m + 1)
                need(pe, s_gte, m * 2)
                for g in range(GT):
                    last = pe.transpose(bank[4 + g // 4][:, P * (g % 4):P * (g % 4) + P],
                                        g_sb[:, g].rearrange("p q h -> p (q h)"), ident)
                last.then_inc(s_gt, 1)

            pe.wait_ge(s_n4, 4)
            for i in range(4):
                last = pe.transpose(bank[6][:, P * i:P * i + P], nat4[:, i].rearrange("p a n -> p (a n)"), ident)
            last.then_inc(s_n4t, 1)
            pe.wait_ge(s_hev, KT)

            def stacks(i0, i1):
                bn = b_nat.rearrange("p s n h -> p (s n) h")
                for i in range(i0, i1):
                    need(pe, s_bce, i - 3)
                    for x in range(4):
                        h = 4 * (i % 4) + x
                        src = (bn[:, NS:3 * NS, h], bn[:, 0:2 * NS, h],
                               c_nat[:, h, 0:2, :].rearrange("p s n -> p (s n)"),
                               c_nat[:, h, 1:3, :].rearrange("p s n -> p (s n)"))[i // 4]
                        last = pe.transpose(bank[2 + i % 4][:, P * x:P * x + P], src, ident)
                    last.then_inc(s_bct, 1)

            pe.wait_ge(s_bc, 1)
            stacks(0, 4)
            pe.wait_ge(s_diag, 3)
            for t in range(3):
                last = pe.matmul(bank[7][:, TO[t]:TO[t] + TR[t]], ones_a[0:TR[t], :], diag[0:TR[t], t, 0:TR[t]],
                                 start=True, stop=True)
            last.then_inc(s_rsrow, 1)
            pe.wait_ge(s_cneg, 2)
            stacks(4, 16)
            pe.wait_ge(s_gev, KT)
            u_product(0, 0, 0, 1)
            u_product(1, 1, 0, 1)
            pe.wait_ge(s_bce, 16)
            pe.wait_ge(s_rho, 4)
            g_transpose(0)

            def toeplitz(m, j):
                pe.wait_ge(s_w, m + 1)
                pe.wait_ge(s_rep, m + 1)
                pe.wait_ge(s_sev, m + 1)
                for g in range(GT):
                    dst = bank[2 + g // 4][:, P * (g % 4):P * (g % 4) + P]
                    rep = b_rep[:, g].rearrange("p q h -> p (q h)")
                    w = w_sb[j % 2][:, g]
                    pe.matmul(dst, rep[:, H:H + P], w[:, 0:L, :].rearrange("p q h -> p (q h)"),
                              start=True, stop=False, skip_group_check=True)
                    last = pe.matmul(dst[:, H:P], rep[:, 0:P], w[:, 0:L - 1, :].rearrange("p q h -> p (q h)"),
                                     start=False, stop=True, skip_group_check=True)
                last.then_inc(s_t, 1)

            def s_product(m, j, g):
                if g == 0:
                    pe.wait_ge(s_uch, (m + 1) * (16 * L))
                    pe.wait_ge(s_gte, m * 2 + 2)
                    need(pe, s_tev, m * 8)
                last = pe.matmul(bank[3][:, C * g:C * g + C], gt_sb[:, g], u_ch[j % 4][:, g], start=True, stop=True)
                if g == GT - 1:
                    last.then_inc(s_s, 1)

            def t_product(m, j, g):
                if g == 0:
                    pe.wait_ge(s_tev, m * 8 + 8)
                    need(pe, s_yev, m)
                pe.matmul(bank[7][:, C * g:C * g + C], t_sb[:, g].rearrange("p t h -> p (t h)"),
                          u_ch[j % 4][:, g], start=(g == 0), stop=False, skip_group_check=True)

            for g in range(GT):
                s_product(0, 0, g)
            toeplitz(0, 0)
            g_transpose(1)

            def keep_clock(n):
                for _ in range(n):
                    pe.matmul(bank[0][:, 0:P], ident, ident, start=True, stop=True)

            def tiles(it):
                last_it = isinstance(it, int) and it == 3
                for j in range(4):
                    m = it * 4 + j
                    w = w_sb[j % 2]
                    need(pe, s_xp, m)
                    pe.wait_ge(s_sev, m + 1)
                    pe.matmul(bank[6][:, 0:GT * C], turn, flat(s_sb), start=True, stop=True).then_inc(s_qs, 1)
                    if last_it and j >= 2:
                        pe.wait_ge(s_uev, KT)
                        keep_clock(20 if j == 2 else 14)

                    def between(k):
                        if k == 5:
                            pe.wait_ge(s_zz, m + 1)
                            pe.matmul(bank[6][:, 0:GT * C], turn, flat(zz), start=True, stop=True).then_inc(s_qz, 1)
                        if 4 <= k < 4 + GT and not (last_it and j == 3):
                            s_product(m + 1, j + 1, k - 4)
                        if k >= KT - GT:
                            t_product(m, j, k - (KT - GT))

                    if last_it and j >= 2:
                        for k in range(KT):
                            between(k)
                    else:
                        u_product(m + 2, j, ((j + 2) // 2) % 2, it + ((j + 2) // 4 + 1), between)
                    pe.wait_ge(s_xp, m + 1)
                    for g in range(GT):
                        last = pe.matmul(bank[7][:, C * g:C * g + C],
                                         w[:, g, 1:L + 1, :].rearrange("p t h -> p (t h)"),
                                         x_prev[:, g, 0:C], start=False, stop=True, skip_group_check=True)
                    last.then_inc(s_y, 1)
                    if not (last_it and j == 3):
                        toeplitz(m + 1, j + 1)
                    if not (last_it and j >= 2):
                        g_transpose(m + 2)

            runs(pe, 4, tiles, 1)

            def new_rows(m, j):
                first = isinstance(m, int) and m == 0
                pe.wait_ge(s_new, m + 1)
                need(pe, s_nev, (m - 1) * 2)
                for t in range(3):
                    last = pe.transpose(bank[4 + j % 2][0:TR[t], P * t:P * t + P], h_new[j % 2][:, TO[t]:TO[t] + TR[t]],
                                        ident)
                last.then_inc(s_nps, 1)
                if first:
                    pe.wait_ge(s_gw, 1)
                wr = w_router[:, bass.ds(m, 1), :].rearrange("p a e -> p (a e)")
                for t in range(3):
                    last = pe.matmul(bank[6][0:TR[t], 64 * t:64 * t + EG + E], h_new[j % 2][:, TO[t]:TO[t] + TR[t]],
                                     wr, start=(first and t == 0), stop=(t == 2), skip_group_check=True)
                last.then_inc(s_log, 1)

            def glu_tiles(it):
                for j in range(4):
                    m = it * 4 + j
                    s2 = 2 * (j // 2)
                    need(pe, s_new, m - 1)
                    first = isinstance(m, int) and m == 0
                    parts = [(0, 0, 12), (1, 0, 12), (0, 12, KT), (1, 12, KT)] if first else [(0, 0, KT), (1, 0, KT)]
                    for half, k0, k1 in parts:
                        if k0 == 0:
                            pe.wait_ge(ring[s2 + half], (it + (BEFORE[s2] - 4 + 1)) * 16)
                        for k in range(k0, k1):
                            if first and half == 0 and k % 4 == 0:
                                pe.wait_ge(s_gelu, k // 4 + 1)
                            last = pe.matmul(bank[2 * (j % 2) + half][:, 0:T],
                                             in_slot(s2 + half)[:, k, P * (j % 2):P * (j % 2) + P], zT[:, k, :],
                                             start=(k == 0), stop=(k == KT - 1))
                    last.then_inc(s_glu, 1)
                    if not (isinstance(m, int) and m == 0):
                        new_rows(m - 1, j + 1)

            runs(pe, 4, glu_tiles, 0)
            new_rows(KT - 1, KT - 1)

            pe.wait_ge(s_tri, 1)
            pe.wait_ge(s_new, KT)
            keep_clock(38)
            pe.wait_ge(s_mask, 1)
            for t in range(3):
                for t0 in range(t + 1):
                    left = before if t0 == t else ones
                    last = pe.matmul(bank[7][0:TR[t], E * t:E * t + E], left[0:TR[t0], 0:TR[t]],
                                     hot[0][0:TR[t0], :, t0], start=(t0 == 0), stop=(t0 == t))
            for t0 in range(3):
                last = pe.matmul(bank[7][0:32, E * 3:E * 4], ones[0:TR[t0], 0:32], hot[0][0:TR[t0], :, t0],
                                 start=(t0 == 0), stop=(t0 == 2))
            last.then_inc(s_rank, 1)
            keep_clock(12)

            def gather(r, q, n, xs):
                for x in xs:
                    if x == 0:
                        pe.wait_ge(s_pick, n + 1)
                        need(pe, s_pgte, n)
                        for t in range(3):
                            last = pe.transpose(bank[3][:, TO[t]:TO[t] + TR[t]],
                                                pick_g[0:TR[t], t].rearrange("p a s -> p (a s)"),
                                                ident[0:TR[t], 0:TR[t]])
                        last.then_inc(s_pgt, 1)
                        need(pe, s_acc, (n - (0 if isinstance(q, int) and q == 0 else 1)) * KT)
                    if x >= 2:
                        pe.wait_ge(s_xg, n * 4 + (x - 1))
                    for k in range(4 * x, 4 * x + 4):
                        for t in range(3):
                            last = pe.matmul(bank[6 + x % 2][:, P * (k % 4):P * (k % 4) + P],
                                             xn[0:TR[t], t, P * k:P * k + P],
                                             pick[0:TR[t], t].rearrange("p a s -> p (a s)"),
                                             start=(t == 0), stop=(t == 2))
                    last.then_inc(s_gath, 1)

            def scatter(n, par):
                pe.wait_ge(s_pgte, n + 1)
                pe.wait_ge(s_ye, n * 4 + 4)
                for k in range(KT):
                    if k >= 2:
                        pe.wait_ge(s_acc, n * KT + (k - 1))
                    pe.matmul(bank[6 + k % 2][:, 0:T], y_pair[:, P * k:P * k + P], pick_t[par],
                              start=True, stop=True).then_inc(s_sc, 1)

            def expert_pass(r, whole=True):
                gather(r, 0, r * NPAIR, (0, 1))

                def experts(it, final=False):
                    def full(stage, i):
                        u = 2 * stage + i
                        return ring[u % 8], (r * 24 + it * 3 + (BEFORE[u % 8] + u // 8 + 1)) * 16

                    def gate_up(j):
                        e = r * E + (it * 4 + j)
                        n = r * NPAIR + (it * 2 + j // 2)
                        first = isinstance(it, int) and it == 0 and j == 0
                        pe.wait_ge(s_xg, n * 4 + (2 if first else 4))
                        need(pe, s_guc, e - 1)
                        for half in range(2):
                            if first and half == 1:
                                gather(r, 0, n, (2, 3))
                                pe.wait_ge(s_xg, n * 4 + 4)
                            g = 6 * (j // 2) + 2 * (j % 2) + half
                            for i in range(2):
                                pe.wait_ge(*full(g, i))
                            for k in range(KT // 2):
                                for i in range(2):
                                    last = pe.matmul(bank[j % 2][SL * i:SL * i + SL, :],
                                                     xg[:, KT // 2 * half + k, SL * (j % 2):SL * (j % 2) + SL],
                                                     gu_slot((2 * g + i) % 8)[:, k, :],
                                                     start=(half == 0 and k == 0), stop=(half == 1 and k == KT // 2 - 1))
                            last.then_inc(s_gu, 1)

                    def turn_gate_up(j):
                        e = r * E + (it * 4 + j)
                        pe.wait_ge(s_guc, e + 1)
                        need(pe, s_hid, e)
                        for f in range(FT):
                            last = pe.transpose(bank[2][:, P * f:P * f + P], gu_s[j % 2][:, P * f:P * f + P], ident)
                        last.then_inc(s_gut, 1)

                    def down(pr):
                        n = r * NPAIR + (it * 2 + pr)
                        pe.wait_ge(s_hid, n * 2 + 2)
                        for g in (6 * pr + 4, 6 * pr + 5):
                            for i in range(2):
                                pe.wait_ge(*full(g, i))
                        for c in range(4):
                            need(pe, s_ye, n * 4 + (c - 1))
                            for f in range(FT):
                                for i in range(2):
                                    u = 2 * (6 * pr + 4 + f // 2) + i
                                    last = pe.matmul(bank[4 + c % 2][SL * i:SL * i + SL, :], hid[i][:, f, :],
                                                     dn_slot(u % 8)[:, f % 2, 512 * c:512 * c + 512],
                                                     start=(f == 0), stop=(f == FT - 1))
                            last.then_inc(s_yp, 1)

                    for pr in range(2):
                        q = it * 2 + pr
                        n = r * NPAIR + q
                        gate_up(2 * pr)
                        if not (isinstance(q, int) and q == 0):
                            scatter(n - 1, 1 - pr)
                        turn_gate_up(2 * pr)
                        gate_up(2 * pr + 1)
                        if isinstance(q, int) and q == NPAIR - 1:
                            turn_gate_up(2 * pr + 1)
                            if final:
                                last_down(full)
                                return
                        else:
                            gather(r, q + 1, n + 1, (0, 1))
                            turn_gate_up(2 * pr + 1)
                            gather(r, q + 1, n + 1, (2, 3))
                        down(pr)

                if whole:
                    runs(pe, E // 4, experts, 1)
                    scatter(r * NPAIR + (NPAIR - 1), 1)
                else:
                    runs(pe, E // 4 - 1, experts, 0)
                return experts

            def last_down(full):
                pe.wait_ge(s_acc, (NPAIR - 1) * KT)
                pe.wait_ge(s_guc, E)
                for n in range(12):
                    c, t = n // 3, n % 3
                    need(pe, s_fev, n - 3)
                    for k in range(4 * c, 4 * c + 4):
                        last = pe.transpose(bank[F_BANK[n % 4]][0:TR[t], P * (k % 4):P * (k % 4) + P],
                                            hT[:, k, TO[t]:TO[t] + TR[t]], ident)
                    last.then_inc(s_fps, 1)
                pe.wait_ge(s_hid, E)
                pe.wait_ge(s_pgte, NPAIR)
                pe.wait_ge(s_ye, (NPAIR - 1) * 4)
                for half in range(2):
                    g = 10 + half
                    for i in range(2):
                        pe.wait_ge(*full(g, i))
                    for c in range(4):
                        for f in range(2):
                            for i in range(2):
                                last = pe.matmul(bank[D_BANK[c]][SL * i:SL * i + SL, :], hid[i][:, 2 * half + f, :],
                                                 dn_slot((2 * g + i) % 8)[:, f, 512 * c:512 * c + 512],
                                                 start=(half == 0 and f == 0), stop=(half == 1 and f == 1))
                        if half == 1:
                            last.then_inc(s_yp, 1)
                pe.wait_ge(s_fev, 12)
                for n in range(12):
                    c, t = n // 3, n % 3
                    pe.wait_ge(s_ye, (NPAIR - 1) * 4 + (c + 1))
                    need(pe, s_fadd, n - 3)
                    pe.matmul(bank[F_BANK[n % 4]][0:TR[t], :], pick_t[1][:, TO[t]:TO[t] + TR[t]],
                              y_pair[:, 512 * c:512 * c + 512], start=True, stop=True).then_inc(s_fin, 1)

            experts_0 = expert_pass(0, whole=False)
            pe.wait_ge(s_count, 1)
            most = pe.value_load(count_sb[0:1, 0:1], min_val=0, max_val=T)
            with pe.If(most > SL):
                experts_0(E // 4 - 1)
                scatter(NPAIR - 1, 1)
                with pe.Fori(1, NPASS) as r:
                    expert_pass(r)
                pe.wait_ge(s_moe, 1)
                for n in range(12):
                    t, k0 = n // 4, 4 * (n % 4)
                    need(pe, s_fev, n - 3)
                    for k in range(k0, k0 + 4):
                        last = pe.transpose(bank[n % 4][0:TR[t], P * (k % 4):P * (k % 4) + P],
                                            hT[:, k, TO[t]:TO[t] + TR[t]], ident)
                    last.then_inc(s_fps, 1)
            with pe.Else():
                experts_0(E // 4 - 1, final=True)

        @block.vector
        def _(dve):
            steps = [0]

            def step(ins):
                steps[0] += 1
                ins.then_inc(s_dve, 1)
                dve.wait_ge(s_dve, steps[0])

            def begin(ins):
                ins.then_inc(s_dve, 1)
                steps[0] += 1

            def begun():
                dve.wait_ge(s_dve, steps[0])

            def tt(o, x, y, op):
                step(dve.tensor_tensor(o, x, y, op))

            def ts(o, x, s1, op0, s2=None, op1=None):
                if op1 is None:
                    step(dve.tensor_scalar(o, x, s1, None, op0))
                else:
                    step(dve.tensor_scalar(o, x, s1, s2, op0, op1))

            def stt(o, x, s, y, op0, op1):
                step(dve.scalar_tensor_tensor(out=o, in0=x, scalar=s, in1=y, op0=op0, op1=op1))

            ADD, SUB, MUL, EQ = ALU.add, ALU.subtract, ALU.mult, ALU.is_equal
            sum_sq, inverse, root, rs = stat3

            def rms(n):
                ts(rs, sum_sq, 1.0 / D, MUL, EPS, ADD)
                dve.reciprocal(inverse, rs).then_inc(s_rs, 1)
                dve.wait_ge(s_root, n)
                tt(rs, rs, root, MUL)
                tt(rs, rs, root, MUL)
                ts(rs, rs, -0.5, MUL, 1.5, ADD)
                dve.tensor_tensor(rs, rs, root, MUL).then_inc(s_rsf, 1)
                dve.wait_ge(s_rsf, n)

            dve.wait_ge(s_vec, 16 * 3)
            lr, li = small[0], small[1]
            log_dt, n_, r_, p_, two, dt = (small[2][:, i:i + 1] for i in range(6))
            ts(n_, log_dt, 1.0 / math.log(2.0), MUL, ROUND, ADD)
            ts(n_, n_, ROUND, SUB)
            ts(n_, n_, -126.0, ALU.max, 127.0, ALU.min)
            stt(r_, n_, -0.693359375, log_dt, MUL, ADD)
            stt(r_, n_, 2.12194440e-4, r_, MUL, ADD)
            ts(p_, r_, 1.0 / 5040, MUL, 1.0 / 720, ADD)
            for c in (1.0 / 120, 1.0 / 24, 1.0 / 6, 0.5, 1.0, 1.0):
                ts(p_, p_, r_, MUL, c, ADD)
            ts(two.bitcast(I32), n_, 127.0, ADD, 8388608.0, MUL)
            tt(dt, p_, two, MUL)
            whl, ang = small[3], small[4]
            ts(ang, li, dt, MUL, INV_2PI, MUL)
            ts(whl, ang, ROUND, ADD)
            ts(whl, whl, ROUND, SUB)
            dve.tensor_tensor(ang, ang, whl, SUB).then_inc(s_ang, 1)
            em, y_ = small[7], small[8]
            ts(y_, lr, dt, MUL, EXP_FLOOR, ALU.max)
            ts(y_, y_, 1.0 / 32, MUL)
            ts(em, y_, 1.0 / math.factorial(9), MUL)
            for k in range(8, 0, -1):
                stt(em, em, 1.0 / math.factorial(k), y_, ADD, MUL)
            for _k in range(5):
                stt(em, em, 2.0, em, ADD, MUL)
            sn, hf, cm, cs, mg = small[5], small[6], small[10], small[11], small[12]
            dve.wait_ge(s_trig, 2)
            stt(cm, hf, -2.0, hf, MUL, MUL)
            ts(cs, cm, 1.0, ADD)
            ts(mg, em, 1.0, ADD)
            ar, ai, nr, den, cr, ci, tmp = small[13], small[14], small[15], small[8], small[9], small[3], small[5]
            tt(ar, mg, cs, MUL)
            tt(ai, mg, sn, MUL)
            tt(nr, em, cs, MUL)
            tt(nr, nr, cm, ADD)
            tt(den, lr, lr, MUL)
            tt(tmp, li, li, MUL)
            tt(den, den, tmp, ADD)
            step(dve.reciprocal(den, den))
            tt(cr, nr, lr, MUL)
            tt(tmp, ai, li, MUL)
            tt(cr, cr, tmp, ADD)
            tt(cr, cr, den, MUL)
            tt(ci, ai, lr, MUL)
            tt(tmp, nr, li, MUL)
            tt(ci, ci, tmp, SUB)
            tt(ci, ci, den, MUL)
            for _k in range(3):
                tt(mg, mg, mg, MUL)
            ts(ang, ang, float(L), MUL)
            whl = small[6]
            ts(whl, ang, ROUND, ADD)
            ts(whl, whl, ROUND, SUB)
            tt(ang, ang, whl, SUB)
            for i, v in enumerate((ar, ai, mg, ang)):
                dve.tensor_copy(nat4[:, i], v.unsqueeze(1).broadcast_to((P, 2, NS))).then_inc(s_n4, 1)
            dve.wait_ge(s_par, 16 * 2)
            crb = cr.unsqueeze(2).broadcast_to((P, NS, H))
            cib = ci.unsqueeze(2).broadcast_to((P, NS, H))
            tt(b_nat[:, 0], b_raw[:, 1], cib, MUL)
            tt(b_nat[:, 1], b_raw[:, 0], crb, MUL)
            tt(b_nat[:, 1], b_nat[:, 1], b_nat[:, 0], SUB)
            tt(b_nat[:, 0], b_raw[:, 0], cib, MUL)
            tt(b_nat[:, 2], b_raw[:, 1], crb, MUL)
            tt(b_nat[:, 2], b_nat[:, 2], b_nat[:, 0], ADD)
            dve.tensor_scalar(b_nat[:, 0], b_nat[:, 2], -1.0, None, MUL).then_inc(s_bc, 1)

            dve.wait_ge(s_stat, 1)
            dve.wait_ge(s_sq, 3)
            rms(1)
            dve.wait_ge(s_const, 1)
            for t in range(3):
                dve.tensor_scalar(diag[0:TR[t], t, 0:TR[t]], ident[0:TR[t], 0:TR[t]], rs[0:TR[t], t:t + 1], None,
                                  MUL).then_inc(s_diag, 1)
            rs_row = flat(t1)
            dve.wait_ge(s_rsrow, 1)
            step(dve.tensor_copy(rs_row, bank[7][:, 0:T]))
            dve.wait_ge(s_gains, 16 * 3)
            for k in range(KT):
                dve.wait_ge(s_hev, k + 1)
                dve.scalar_tensor_tensor(out=hsT[:, k, :], in0=hT[:, k, :], scalar=g_mix[:, k:k + 1], in1=rs_row,
                                         op0=MUL, op1=MUL).then_inc(s_gev, 1)

            dve.wait_ge(s_n4t, 1)
            for i, o in enumerate((pow_re[:, 1, :], pow_im[:, 1, :], rho8, phi8)):
                dve.tensor_copy(o, bank[6][:, P * i:P * i + P]).then_inc(s_rho, 1)
            dve.wait_ge(s_rho, 4)
            for base in (1, 2, 4):
                shape = (P, base, G)
                kr = pow_re[:, base:base + 1, :].broadcast_to(shape)
                ki = pow_im[:, base:base + 1, :].broadcast_to(shape)
                xr, xi = pow_re[:, 1:1 + base, :], pow_im[:, 1:1 + base, :]
                o_re, o_im = pow_re[:, base + 1:2 * base + 1, :], pow_im[:, base + 1:2 * base + 1, :]
                tm = p_tmp[:, 0:base, :]
                tt(o_re, kr, xr, MUL)
                tt(tm, ki, xi, MUL)
                tt(o_re, o_re, tm, SUB)
                tt(o_im, kr, xi, MUL)
                tt(tm, ki, xr, MUL)
                tt(o_im, o_im, tm, ADD)
            step(dve.memset(pow_re[:, 0, :], 1.0))
            dve.memset(pow_im[:, 0, :], 0.0).then_inc(s_pow, 1)
            dve.wait_ge(s_pow, 1)
            dve.wait_ge(s_bce, 16)

            def w_of(m, j):
                full = (P, GT, L + 1, H)
                g0 = bass.ds(m * GT, GT)
                pr = pow_re[:, :, g0].rearrange("p q g -> p g q").unsqueeze(3).broadcast_to(full)
                pi = pow_im[:, :, g0].rearrange("p q g -> p g q").unsqueeze(3).broadcast_to(full)
                v1 = c1[:, :, g0].rearrange("p h g -> p g h").unsqueeze(2).broadcast_to(full)
                v2 = c2[:, :, g0].rearrange("p h g -> p g h").unsqueeze(2).broadcast_to(full)
                dve.tensor_tensor(w_tmp, v2, pi, MUL).then_inc(s_wt, 1)
                need(dve, s_y, m - 1)
                dve.tensor_tensor(w_sb[j % 2], v1, pr, MUL).then_inc(s_wt, 1)
                dve.wait_ge(s_wt, m * 2 + 2)
                dve.tensor_tensor(w_sb[j % 2], w_sb[j % 2], w_tmp, ADD).then_inc(s_w, 1)

            def z_of(m):
                return zT[:, bass.ds(m, 1), :].rearrange("p a t -> p (a t)")

            def d_times_u(m, j):
                dve.wait_ge(s_uev, m + 1)
                dve.tensor_scalar(z_of(m), u_sb[j % 2], d_skip[:, bass.ds(m, 1)], None, MUL).then_inc(s_du, 1)

            def y_add(m, j):
                dve.wait_ge(s_ych, (m + 1) * (16 * GT))
                dve.wait_ge(s_du, m + 1)
                dve.tensor_tensor(z_of(m), z_of(m), y_ch[j % 2], ADD).then_inc(s_z, 1)

            def tiles(it):
                last = isinstance(it, int) and it == 3
                for j in range(4):
                    m = it * 4 + j
                    turned = bank[6][:, 0:GT * C]
                    cos_m, sin_m = flat(cos_t[j % 2]), flat(sin_t[j % 2])
                    dve.wait_ge(s_tab, m + 1)
                    dve.wait_ge(s_sev, m + 1)
                    dve.tensor_tensor(flat(t1), cos_m, flat(s_sb), MUL).then_inc(s_ch, 1)
                    dve.wait_ge(s_qs, m + 1)
                    dve.tensor_tensor(flat(t2), sin_m, turned, MUL).then_inc(s_ch, 1)
                    dve.wait_ge(s_ch, m * 5 + 2)
                    dve.tensor_tensor(flat(t1), flat(t1), flat(t2), ADD).then_inc(s_ch, 1)
                    dve.wait_ge(s_ch, m * 5 + 3)
                    dve.wait_ge(s_tp, m * 4 + 4)
                    dve.tensor_tensor_scan(flat(zz), flat(mag_t[j % 2]), flat(t1), 0.0, MUL, ADD).then_inc(s_zz, 1)
                    dve.wait_ge(s_zz, m + 1)
                    dve.tensor_tensor(flat(t1), cos_m, flat(zz), MUL).then_inc(s_ch, 1)
                    dve.wait_ge(s_qz, m + 1)
                    dve.tensor_tensor(flat(t2), sin_m, turned, MUL).then_inc(s_ch, 1)
                    dve.wait_ge(s_ch, m * 5 + 5)
                    if isinstance(m, int) and m == 0:
                        dve.wait_ge(s_x0, 1)
                    dve.tensor_tensor(x_prev[:, :, 1:C + 1], t1, t2, SUB).then_inc(s_xp, 1)
                    if not (last and j == 3):
                        w_of(m + 1, j + 1)
                    if not (last and j >= 2):
                        d_times_u(m + 2, j)
                    if not (isinstance(m, int) and m == 0):
                        y_add(m - 1, j + 1)

            w_of(0, 0)
            d_times_u(0, 0)
            d_times_u(1, 1)
            runs(dve, 4, tiles, 1)
            y_add(KT - 1, KT - 1)

            dve.memset(sumsq, 0.0).then_inc(s_ssz, 1)
            dve.wait_ge(s_router, 16 * 4)
            dve.tensor_tensor(w_router, w_router, g_ffn.unsqueeze(2).broadcast_to((P, KT, EG + E)), MUL
                              ).then_inc(s_gw, 1)

            def to_rows(m, j):
                dve.wait_ge(s_nps, m + 1)
                src = bank[4 + j % 2][:, 0:3 * P].rearrange("p (t c) -> p t c", t=3)
                cols = bass.ds(m * P, P)
                dve.tensor_copy(xn[0:R, 0:2, cols], src[0:R, 0:2, :]).then_inc(s_nev, 1)
                dve.tensor_copy(xn[0:TR[2], 2, cols], src[0:TR[2], 2, :]).then_inc(s_nev, 1)

            def glu_tiles(it):
                for j in range(4):
                    m = it * 4 + j
                    dve.wait_ge(s_sig, m + 1)
                    need(dve, s_new, m)
                    dve.tensor_tensor(value_s, bank[2 * (j % 2)][:, 0:T], gate_s[j % 2], MUL).then_inc(s_gl, 1)
                    dve.wait_ge(s_gl, m + 1)
                    need(dve, s_res, m - 1)
                    need(dve, s_log, m - 1)
                    dve.tensor_tensor(h_new[j % 2], value_s, hT[:, bass.ds(m, 1), :].rearrange("p a t -> p (a t)"),
                                      ADD).then_inc(s_new, 1)
                    if not (isinstance(m, int) and m == 0):
                        to_rows(m - 1, j + 1)

            runs(dve, 4, glu_tiles, 0)
            to_rows(KT - 1, KT - 1)

            begin(dve.memset(logit, 0.0))
            begin(dve.memset(coarse, -3.0e38))
            begin(dve.memset(gates, 0.0))
            begin(dve.memset(rank, -1.0))
            begun()
            dve.wait_ge(s_ssp, 3 * KT)
            step(dve.tensor_reduce(sum_sq, sumsq[0:R], AX.X, ADD))
            rms(2)
            dve.wait_ge(s_nev, 2 * KT)
            dve.wait_ge(s_log, KT)
            for t in range(3):
                rows = slice(0, TR[t])
                begin(dve.scalar_tensor_tensor(out=logit[rows, t, :], in0=bank[6][rows, 64 * t:64 * t + EG + E],
                                               scalar=rs[rows, t:t + 1], in1=b_router[rows, :], op0=MUL, op1=ADD))
            begun()
            rows = slice(0, R)
            three = lambda v, n: v[rows].unsqueeze(2).broadcast_to((R, 3, n))
            step(dve.tensor_copy(coarse[rows, :, 0:EG], logit[rows, :, 0:EG]))
            for t in range(3):
                begin(dve.max(cmax[rows, t, :], coarse[rows, t, :]))
            begun()
            for t in range(3):
                begin(dve.max_index(cidx[rows, t, :], cmax[rows, t, :], coarse[rows, t, :]))
            begun()
            dve.tensor_tensor(ex4[rows], logit[rows, :, 0:EG], cmax[rows, :, 0:1].broadcast_to((R, 3, EG)), SUB
                              ).then_inc(s_rt, 1)
            p_group, group, w0, w1, e0, e1, i0, i1, tot = (col[i] for i in (0, 1, 4, 5, 6, 7, 8, 9, 10))
            diff = col[3]
            step(dve.tensor_copy(group[rows].unsqueeze(2), cidx[rows, :, 0:1]))
            tt(one4[rows], iota[rows, 0:EG].unsqueeze(1).broadcast_to((R, 3, EG)), three(group, EG), EQ)
            for t in range(3):
                begin(dve.tensor_tensor(prod[rows, t], logit[rows, t, EG:].rearrange("p (g e) -> p e g", g=EG),
                                        one4[rows, t].unsqueeze(1).broadcast_to((R, EL, EG)), MUL))
            begun()
            step(dve.tensor_reduce(fine_sel[rows], prod[rows], AX.X, ADD))
            for t in range(3):
                begin(dve.max(fmax[rows, t, :], fine_sel[rows, t, :]))
            begun()
            for t in range(3):
                begin(dve.max_index(fidx[rows, t, :], fmax[rows, t, :], fine_sel[rows, t, :]))
            begun()
            dve.tensor_tensor(diff[rows].unsqueeze(2), fmax[rows, :, 1:2], fmax[rows, :, 0:1], SUB).then_inc(s_rt, 1)
            begin(dve.tensor_copy(i0[rows].unsqueeze(2), fidx[rows, :, 0:1]))
            begin(dve.tensor_copy(i1[rows].unsqueeze(2), fidx[rows, :, 1:2]))
            begun()
            for e_, i_ in ((e0, i0), (e1, i1)):
                begin(dve.scalar_tensor_tensor(out=e_[rows], in0=group[rows], scalar=float(EL), in1=i_[rows],
                                               op0=MUL, op1=ADD))
            begun()
            many = lambda v: v[rows].unsqueeze(1).broadcast_to((R, E, 3))
            experts_i = iota[rows, 0:E].unsqueeze(2).broadcast_to((R, E, 3))
            begin(dve.tensor_tensor(hot[1][rows], experts_i, many(e0), EQ))
            begin(dve.tensor_tensor(hot[2][rows], experts_i, many(e1), EQ))
            begun()
            dve.tensor_tensor(hot[0][rows], hot[1][rows], hot[2][rows], ADD).then_inc(s_mask, 1)
            dve.wait_ge(s_ex, 1)
            step(dve.tensor_reduce(tot[rows], ex4[rows], AX.X, ADD))
            step(dve.reciprocal(p_group[rows], tot[rows]))
            dve.wait_ge(s_ex, 2)
            ts(tot[rows], diff[rows], 1.0, ADD)
            step(dve.reciprocal(w0[rows], tot[rows]))
            tt(w0[rows], w0[rows], p_group[rows], MUL)
            begin(dve.tensor_tensor(w1[rows], w0[rows], diff[rows], MUL))
            begin(dve.tensor_tensor(hot[1][rows], hot[1][rows], many(w0), MUL))
            begun()
            dve.wait_ge(s_mask, 1)
            tt(hot[2][rows], hot[2][rows], many(w1), MUL)
            tt(gates[rows, 0:E, :], hot[1][rows], hot[2][rows], ADD)
            dve.wait_ge(s_rank, 1)
            for t in range(3):
                rw = slice(0, TR[t])
                begin(dve.scalar_tensor_tensor(out=rank[rw, 0:E, t], in0=bank[7][rw, E * t:E * t + E], scalar=1.0,
                                               in1=hot[0][rw, :, t], op0=ADD, op1=MUL))
            begin(dve.tensor_reduce(tot[0:1, 0:1], bank[7][0:1, E * 3:E * 4], AX.X, ALU.max))
            begun()
            ts(rank[rows], rank[rows], -1.0, ADD)
            dve.tensor_copy(count_sb[0:1, 0:1], tot[0:1, 0:1]).then_inc(s_count, 1)
            dve.wait_ge(s_count, 1)
            dve.wait_ge(s_res, KT)

            def picks(r, q):
                n = r * NPAIR + q
                need(dve, s_gath, n * 4)
                two_e = bass.ds(q * 2, 2)
                full = (R, 3, 2, SL)
                slots = iota[rows].unsqueeze(1).unsqueeze(1).broadcast_to(full)
                ranks = rank[rows, two_e, :].rearrange("p e t -> p t e").unsqueeze(3).broadcast_to(full)
                weights = gates[rows, two_e, :].rearrange("p e t -> p t e").unsqueeze(3).broadcast_to(full)
                dve.tensor_tensor(pick[rows], slots, ranks, EQ).then_inc(s_pk, 1)
                dve.wait_ge(s_pk, n * 2 + 1)
                dve.tensor_tensor(pick_g[rows], pick[rows], weights, MUL).then_inc(s_pk, 1)
                dve.wait_ge(s_pk, n * 2 + 2)
                scales = rs[rows].unsqueeze(2).unsqueeze(3).broadcast_to(full)
                dve.tensor_tensor(pick[rows], pick[rows], scales, MUL).then_inc(s_pick, 1)

            def gathered(n, par, xs):
                for x in xs:
                    if x == 0:
                        dve.wait_ge(s_pgt, n + 1)
                        dve.tensor_copy(pick_t[par], bank[3][:, 0:T]).then_inc(s_pgte, 1)
                    dve.wait_ge(s_gath, n * 4 + (x + 1))
                    dve.tensor_tensor(xg[:, 4 * x:4 * x + 4, :],
                                      bank[6 + x % 2][:, :].rearrange("p (k s) -> p k s", k=4),
                                      g_ffn[:, 4 * x:4 * x + 4].unsqueeze(2).broadcast_to((P, 4, 2 * SL)), MUL
                                      ).then_inc(s_xg, 1)

            def add_pair(n):
                for k in range(KT):
                    dve.wait_ge(s_sc, n * KT + (k + 1))
                    dve.tensor_tensor(hT[:, k, :], hT[:, k, :], bank[6 + k % 2][:, 0:T], ADD).then_inc(s_acc, 1)

            def hidden(e, j):
                dve.wait_ge(s_silu, e + 1)
                dve.tensor_tensor(hid[j], silu_s, bank[2][:, :].rearrange("p (f s) -> p f s", f=FT)[:, :, SL:], MUL
                                  ).then_inc(s_hid, 1)

            def expert_pass(r, whole=True):
                picks(r, 0)
                gathered(r * NPAIR, 0, range(4))

                def experts(it):
                    for pr in range(2):
                        q = it * 2 + pr
                        n = r * NPAIR + q
                        more = not (isinstance(q, int) and q == NPAIR - 1)
                        if more:
                            picks(r, q + 1)
                        if not (isinstance(q, int) and q == 0):
                            add_pair(n - 1)
                        hidden(n * 2, 0)
                        if more:
                            gathered(n + 1, 1 - pr, (0, 1))
                        hidden(n * 2 + 1, 1)
                        if more:
                            gathered(n + 1, 1 - pr, (2, 3))

                if whole:
                    runs(dve, E // 4, experts, 1)
                    add_pair(r * NPAIR + (NPAIR - 1))
                else:
                    runs(dve, E // 4 - 1, experts, 0)
                return experts

            s_pk, s_less = sem("pick_step"), sem("ranks_lowered")
            step(dve.memset(fin_sq, 0.0))
            experts_0 = expert_pass(0, whole=False)
            most = dve.value_load(count_sb[0:1, 0:1], min_val=0, max_val=T)
            base = steps[0]
            with dve.If(most > SL):
                experts_0(E // 4 - 1)
                add_pair(NPAIR - 1)
                with dve.Fori(1, NPASS) as r:
                    dve.tensor_scalar(rank, rank, -float(SL), None, ADD).then_inc(s_less, 1)
                    dve.wait_ge(s_less, r)
                    expert_pass(r)
                dve.wait_ge(s_acc, NPASS * NPAIR * KT)
                dve.memset(pick_t[1], 0.0).then_inc(s_moe, 1)
                for n in range(12):
                    t, k0 = n // 4, 4 * (n % 4)
                    dve.wait_ge(s_fps, n + 1)
                    dve.tensor_copy(xn[0:TR[t], t, P * k0:P * (k0 + 4)], bank[n % 4][0:TR[t], :]).then_inc(s_fev, 1)
                dve.wait_ge(s_fsq, 3)
                rms(3)
                dve.wait_ge(s_gf, 16)
                for t in range(3):
                    dve.scalar_tensor_tensor(out=f_out[0:TR[t], t, :], in0=xn[0:TR[t], t, :],
                                             scalar=rs[0:TR[t], t:t + 1], in1=g_final[0:TR[t]],
                                             op0=MUL, op1=MUL).then_inc(s_o, 1)
            with dve.Else():
                steps[0] = base
                experts_0(E // 4 - 1)
                dve.wait_ge(s_fev, 12)
                dve.wait_ge(s_gf, 16)

                def gained(n):
                    c, t = n // 3, n % 3
                    part = slice(512 * c, 512 * c + 512)
                    dve.tensor_tensor(f_out[0:TR[t], t, part], xn[0:TR[t], t, part], g_final[0:TR[t], part], MUL
                                      ).then_inc(s_scaled, 1)

                for n in range(12):
                    c, t = n // 3, n % 3
                    x = xn[0:TR[t], t, 512 * c:512 * c + 512]
                    dve.wait_ge(s_fin, n + 1)
                    dve.tensor_tensor(x, x, bank[F_BANK[n % 4]][0:TR[t], :], ADD).then_inc(s_fadd, 1)
                    if 3 <= n < 6:
                        dve.wait_ge(s_fadd, n - 2)
                        gained(n - 3)
                dve.wait_ge(s_fadd, 6)
                for n in range(3, 6):
                    gained(n)
                dve.wait_ge(s_fsq, 12)
                step(dve.tensor_reduce(sum_sq, fin_sq[0:R], AX.X, ADD))
                rms(3)
                half = slice(D // 2, D)
                for t in range(3):
                    dve.scalar_tensor_tensor(out=f_out[0:TR[t], t, half], in0=xn[0:TR[t], t, half],
                                             scalar=rs[0:TR[t], t:t + 1], in1=g_final[0:TR[t], half],
                                             op0=MUL, op1=MUL).then_inc(s_o, 1)


_INS = ["x", "meta_tokens", "norm_mix", "norm_ffn", "norm_final", "s5_w_in", "s5_a_re", "s5_a_im", "s5_log_dt",
        "s5_b_re", "s5_b_im", "s5_c_re", "s5_c_im", "s5_d", "s5_w_glu", "moe_w_coarse", "moe_b_coarse",
        "moe_w_fine", "moe_b_fine", "moe_w_gate", "moe_w_up", "moe_w_down"]


def kernel(**inputs):
    import numpy as _np
    import concourse.bacc as _bacc
    from concourse import mybir as _mybir
    from concourse.bass_utils import run_bass_kernel_spmd as _run

    nc = _bacc.Bacc("TRN2", target_bir_lowering=False, num_devices=1)
    arrays, args = {}, {}
    for name in _INS:
        v = _np.ascontiguousarray(inputs[name])
        arrays[f"in_{name}"] = v
        args[name] = nc.dram_tensor(f"in_{name}", v.shape, _mybir.dt.from_np(v.dtype), kind="ExternalInput").ap()
    out = nc.dram_tensor("out_0", (1, SEQ, D), F32, kind="ExternalOutput").ap()
    trunk(nc, args, out)
    r = _run(nc, [arrays], core_ids=[0])
    return r.results[0]["out_0"]
```
